# Optimizing a Trainium2 kernel written in Bass

```python
import math
import jax
import jax.numpy as jnp
from jax import lax
import numpy as np

D_MODEL = 2048
BATCH = 1
SEQ = 256
DEPTH = 2

MEM_LEN = 256
EPS = 1e-6
GDN_HEADS = 8
GDN_DK = 128
GDN_DV = 128
GDN_CONV = 4
GDN_CHUNK = 64
LRU_WIDTH = D_MODEL // 2
LRU_BLOCKS = 8
LRU_BLOCK = LRU_WIDTH // LRU_BLOCKS
LRU_CONV = 4
LRU_C = 8.0
SWA_HEADS = 32
SWA_KV_HEADS = 8
SWA_GROUP = SWA_HEADS // SWA_KV_HEADS
SWA_HD = 64
SWA_WINDOW = 128
SWA_BLOCK = 128
ROPE_THETA = 10000.0
X_HEADS = 4
X_HD = 128
D_FF = 5632
FFN_CONV = 3

GDN_QK = GDN_HEADS * GDN_DK
GDN_V = GDN_HEADS * GDN_DV
GDN_QKV = 2 * GDN_QK + GDN_V
HYB_SIZES = (GDN_QKV, GDN_V, GDN_HEADS, GDN_HEADS, LRU_WIDTH, LRU_WIDTH)
HYB_IN = GDN_QKV + GDN_V + 2 * GDN_HEADS + 2 * LRU_WIDTH
HYB_MIX = GDN_V + LRU_WIDTH
SWA_Q = SWA_HEADS * SWA_HD
SWA_KV = SWA_KV_HEADS * SWA_HD
SWA_SIZES = (SWA_Q, SWA_KV, SWA_KV)
SWA_IN = SWA_Q + 2 * SWA_KV
X_INNER = X_HEADS * X_HD
N_EVEN = (DEPTH + 1) // 2
N_ODD = DEPTH // 2

kernel_name = 'hybrid_gdn_rglru_swa_trunk'

def split_cols(t, sizes):
    out, start = [], 0
    for s in sizes:
        out.append(t[..., start:start + s])
        start += s
    return out

def rmsnorm(x, g):
    xf = x.astype(jnp.float32)
    y = xf * lax.rsqrt(jnp.mean(xf * xf, axis=-1, keepdims=True) + EPS)
    return (y * g.astype(jnp.float32)).astype(x.dtype)

def causal_dwconv(x, w):
    width, ch = w.shape
    return lax.conv_general_dilated(
        x, w[:, None, :].astype(x.dtype), window_strides=(1,), padding=((width - 1, 0),),
        dimension_numbers=('NWC', 'WIO', 'NWC'), feature_group_count=ch)

def rope_tables(positions, dim):
    inv = 1.0 / (ROPE_THETA ** (jnp.arange(0, dim, 2, dtype=jnp.float32) / dim))
    ang = positions.astype(jnp.float32)[..., None] * inv
    return jnp.cos(ang), jnp.sin(ang)

def apply_rope(x, cos, sin):
    xf = x.astype(jnp.float32)
    x1, x2 = jnp.split(xf, 2, axis=-1)
    c, s = cos[:, :, None, :], sin[:, :, None, :]
    return jnp.concatenate([x1 * c - x2 * s, x2 * c + x1 * s], axis=-1).astype(x.dtype)

def gated_delta_rule(q, k, v, g, beta):
    b, s, h, dk = q.shape
    dv = v.shape[-1]
    c = GDN_CHUNK
    n = s // c

    def blocks(t):
        t = t.astype(jnp.float32).reshape((b, n, c, h) + t.shape[3:])
        return jnp.moveaxis(t, 3, 1)

    q = blocks(q) * (dk ** -0.5)
    k, v, g, beta = blocks(k), blocks(v), blocks(g), blocks(beta)
    gc = jnp.cumsum(g, axis=-1)
    causal = jnp.tril(jnp.ones((c, c), dtype=bool))
    strict = jnp.tril(jnp.ones((c, c), dtype=bool), -1)
    decay = jnp.exp(jnp.where(causal, gc[..., :, None] - gc[..., None, :], -jnp.inf))
    kb = k * beta[..., None]
    l_mat = jnp.where(strict, jnp.einsum('bhnik,bhnjk->bhnij', kb, k) * decay, 0.0)
    eye = jnp.eye(c, dtype=jnp.float32)
    tmat = lax.linalg.triangular_solve(eye + l_mat, jnp.broadcast_to(eye, l_mat.shape),
                                       left_side=True, lower=True, unit_diagonal=True)
    u = jnp.einsum('bhnij,bhnjd->bhnid', tmat, v * beta[..., None])
    w = jnp.einsum('bhnij,bhnjd->bhnid', tmat, kb * jnp.exp(gc)[..., None])
    attn = jnp.where(causal, jnp.einsum('bhnik,bhnjk->bhnij', q, k) * decay, 0.0)
    q_dec = q * jnp.exp(gc)[..., None]
    g_last = gc[..., -1]
    k_dec = k * jnp.exp(g_last[..., None] - gc)[..., None]

    def step(state, inp):
        u_i, w_i, a_i, qd_i, kd_i, gl_i = inp
        v_new = u_i - jnp.einsum('bhck,bhkv->bhcv', w_i, state)
        o_i = jnp.einsum('bhck,bhkv->bhcv', qd_i, state) + jnp.einsum('bhcj,bhjv->bhcv', a_i, v_new)
        state = state * jnp.exp(gl_i)[..., None, None] + jnp.einsum('bhck,bhcv->bhkv', kd_i, v_new)
        return state, o_i

    xs = tuple(jnp.moveaxis(t, 2, 0) for t in (u, w, attn, q_dec, k_dec, g_last))
    state0 = jnp.zeros((b, h, dk, dv), jnp.float32)
    _, o = lax.scan(step, state0, xs)
    return jnp.transpose(o, (1, 0, 3, 2, 4)).reshape(b, s, h, dv)

def gdn_mixer(qkv, z, b_raw, a_raw, conv_w, a_log, dt_bias, norm_g):
    bsz, s, _ = qkv.shape
    qkv_c = jax.nn.silu(causal_dwconv(qkv, conv_w))
    q, k, v = split_cols(qkv_c, (GDN_QK, GDN_QK, GDN_V))

    def heads(t, d):
        return t.reshape(bsz, s, GDN_HEADS, d).astype(jnp.float32)

    def l2n(t):
        return t * lax.rsqrt(jnp.sum(t * t, axis=-1, keepdims=True) + EPS)

    q, k, v = l2n(heads(q, GDN_DK)), l2n(heads(k, GDN_DK)), heads(v, GDN_DV)
    beta = jax.nn.sigmoid(b_raw.astype(jnp.float32))
    g = -jnp.exp(a_log.astype(jnp.float32)) * jax.nn.softplus(
        a_raw.astype(jnp.float32) + dt_bias.astype(jnp.float32))
    o = gated_delta_rule(q, k, v, g, beta)
    o = rmsnorm(o, norm_g) * jax.nn.silu(heads(z, GDN_DV))
    return o.reshape(bsz, s, GDN_V).astype(qkv.dtype)

def rglru_mixer(xr, gate, conv_w, conv_b, w_r, b_r, w_i, b_i, lam):
    bsz, s, _ = xr.shape
    xc = (causal_dwconv(xr, conv_w) + conv_b).astype(jnp.float32)
    xh = xc.reshape(bsz, s, LRU_BLOCKS, LRU_BLOCK)
    r = jax.nn.sigmoid(jnp.einsum('bshi,hij->bshj', xh, w_r.astype(jnp.float32)).reshape(bsz, s, LRU_WIDTH)
                       + b_r.astype(jnp.float32))
    i = jax.nn.sigmoid(jnp.einsum('bshi,hij->bshj', xh, w_i.astype(jnp.float32)).reshape(bsz, s, LRU_WIDTH)
                       + b_i.astype(jnp.float32))
    log_a = -LRU_C * r * jax.nn.softplus(-lam.astype(jnp.float32))
    a = jnp.exp(log_a)
    inp = jnp.sqrt(-jnp.expm1(2.0 * log_a)) * (i * xc)

    def combine(lhs, rhs):
        a_l, h_l = lhs
        a_r, h_r = rhs
        return a_l * a_r, a_r * h_l + h_r

    _, hseq = lax.associative_scan(combine, (a, inp), axis=1)
    return hseq.astype(xr.dtype) * jax.nn.gelu(gate)

def swa_mixer(qkv, q_norm, k_norm, sinks, cos, sin):
    bsz, s, _ = qkv.shape
    q, k, v = split_cols(qkv, SWA_SIZES)
    q = apply_rope(rmsnorm(q.reshape(bsz, s, SWA_HEADS, SWA_HD), q_norm), cos, sin)
    k = apply_rope(rmsnorm(k.reshape(bsz, s, SWA_KV_HEADS, SWA_HD), k_norm), cos, sin)
    v = v.reshape(bsz, s, SWA_KV_HEADS, SWA_HD)
    blk = SWA_BLOCK
    nb = s // blk
    qb = q.reshape(bsz, nb, blk, SWA_KV_HEADS, SWA_GROUP, SWA_HD)

    def band(t):
        tp = jnp.pad(t, ((0, 0), (blk, 0), (0, 0), (0, 0))).reshape(bsz, nb + 1, blk, SWA_KV_HEADS, SWA_HD)
        return jnp.concatenate([tp[:, :-1], tp[:, 1:]], axis=2)

    kb, vb = band(k), band(v)
    sc = jnp.einsum('bnqkgd,bnjkd->bnkgqj', qb, kb).astype(jnp.float32) * (SWA_HD ** -0.5)
    qi = jnp.arange(blk)[:, None]
    kj = jnp.arange(2 * blk)[None, :]
    rel = blk + qi - kj
    bidx = jnp.arange(nb)[:, None, None]
    valid = (rel >= 0) & (rel < SWA_WINDOW) & (bidx * blk + kj - blk >= 0)
    sc = jnp.where(valid[None, :, None, None], sc, -jnp.inf)
    sink = sinks.astype(jnp.float32).reshape(SWA_KV_HEADS, SWA_GROUP)[None, None, :, :, None, None]
    m = jnp.maximum(jnp.max(sc, axis=-1, keepdims=True), sink)
    p = jnp.exp(sc - m)
    denom = jnp.sum(p, axis=-1, keepdims=True) + jnp.exp(sink - m)
    o = jnp.einsum('bnkgqj,bnjkd->bnqkgd', p / denom, vb.astype(jnp.float32))
    return o.reshape(bsz, s, SWA_Q).astype(qkv.dtype)

def cross_attn(h, mem_n, wq, wkv, wo, q_norm, k_norm):
    bsz, s, _ = h.shape
    q = rmsnorm((h @ wq).reshape(bsz, s, X_HEADS, X_HD), q_norm)
    k, v = split_cols(mem_n @ wkv, (X_INNER, X_INNER))
    k = rmsnorm(k.reshape(bsz, MEM_LEN, X_HEADS, X_HD), k_norm)
    v = v.reshape(bsz, MEM_LEN, X_HEADS, X_HD)
    sc = jnp.einsum('bshd,bmhd->bhsm', q, k).astype(jnp.float32) * (X_HD ** -0.5)
    p = jax.nn.softmax(sc, axis=-1).astype(v.dtype)
    o = jnp.einsum('bhsm,bmhd->bshd', p, v).reshape(bsz, s, X_INNER)
    return o @ wo

def conv_ffn(h, w_in, conv_w, conv_b, w_out):
    gt, up = split_cols(h @ w_in, (D_FF, D_FF))
    gt = causal_dwconv(gt, conv_w) + conv_b
    return (jax.nn.silu(gt) * up) @ w_out

def setup_inputs(seed: int = 0) -> dict:
    key = jax.random.key(seed)
    ks = iter(jax.random.split(key, 48))
    f32 = jnp.float32
    D, L, E, O = D_MODEL, DEPTH, N_EVEN, N_ODD

    def nrm(shape, scale):
        return jax.random.normal(next(ks), shape, f32) * scale

    def gain(shape):
        return 1.0 + nrm(shape, 0.02)

    x = nrm((BATCH, SEQ, D), 1.0)
    mem = nrm((BATCH, MEM_LEN, D), 1.0)
    positions = (jax.random.randint(next(ks), (BATCH, 1), 0, 1024) + jnp.arange(SEQ)[None, :]).astype(jnp.int32)
    norm_mix = gain((L, D))
    norm_cross = gain((L, D))
    norm_mem = gain((L, D))
    norm_ffn = gain((L, D))
    xq_w = nrm((L, D, X_INNER), D ** -0.5)
    xkv_w = nrm((L, D, 2 * X_INNER), D ** -0.5)
    xo_w = nrm((L, X_INNER, D), X_INNER ** -0.5)
    xq_norm = gain((L, X_HD))
    xk_norm = gain((L, X_HD))
    ffn_in_w = nrm((L, D, 2 * D_FF), D ** -0.5)
    ffn_conv_w = nrm((L, FFN_CONV, D_FF), FFN_CONV ** -0.5)
    ffn_conv_b = nrm((L, D_FF), 0.02)
    ffn_out_w = nrm((L, D_FF, D), D_FF ** -0.5)
    hyb_in_w = nrm((E, D, HYB_IN), D ** -0.5)
    hyb_out_w = nrm((E, HYB_MIX, D), HYB_MIX ** -0.5)
    gdn_conv_w = nrm((E, GDN_CONV, GDN_QKV), GDN_CONV ** -0.5)
    gdn_a_log = jnp.log(jax.random.uniform(next(ks), (E, GDN_HEADS), f32, 1.0, 16.0))
    dt = jnp.exp(jax.random.uniform(next(ks), (E, GDN_HEADS), f32, math.log(1e-3), math.log(1e-1)))
    gdn_dt_bias = dt + jnp.log(-jnp.expm1(-dt))
    gdn_norm = gain((E, GDN_DV))
    lru_conv_w = nrm((E, LRU_CONV, LRU_WIDTH), LRU_CONV ** -0.5)
    lru_conv_b = nrm((E, LRU_WIDTH), 0.02)
    lru_wr = nrm((E, LRU_BLOCKS, LRU_BLOCK, LRU_BLOCK), LRU_BLOCK ** -0.5)
    lru_br = nrm((E, LRU_WIDTH), 0.02)
    lru_wi = nrm((E, LRU_BLOCKS, LRU_BLOCK, LRU_BLOCK), LRU_BLOCK ** -0.5)
    lru_bi = nrm((E, LRU_WIDTH), 0.02)
    a0 = jax.random.uniform(next(ks), (E, LRU_WIDTH), f32, 0.9, 0.999) ** (1.0 / LRU_C)
    lru_lambda = jnp.log(a0) - jnp.log1p(-a0)
    swa_in_w = nrm((O, D, SWA_IN), D ** -0.5)
    swa_out_w = nrm((O, SWA_Q, D), SWA_Q ** -0.5)
    swa_q_norm = gain((O, SWA_HD))
    swa_k_norm = gain((O, SWA_HD))
    swa_sinks = nrm((O, SWA_HEADS), 0.5)
    return {
        'x': x, 'mem': mem, 'positions': positions,
        'norm_mix': norm_mix, 'norm_cross': norm_cross, 'norm_mem': norm_mem, 'norm_ffn': norm_ffn,
        'xq_w': xq_w, 'xkv_w': xkv_w, 'xo_w': xo_w, 'xq_norm': xq_norm, 'xk_norm': xk_norm,
        'ffn_in_w': ffn_in_w, 'ffn_conv_w': ffn_conv_w, 'ffn_conv_b': ffn_conv_b, 'ffn_out_w': ffn_out_w,
        'hyb_in_w': hyb_in_w, 'hyb_out_w': hyb_out_w,
        'gdn_conv_w': gdn_conv_w, 'gdn_a_log': gdn_a_log, 'gdn_dt_bias': gdn_dt_bias, 'gdn_norm': gdn_norm,
        'lru_conv_w': lru_conv_w, 'lru_conv_b': lru_conv_b, 'lru_wr': lru_wr, 'lru_br': lru_br,
        'lru_wi': lru_wi, 'lru_bi': lru_bi, 'lru_lambda': lru_lambda,
        'swa_in_w': swa_in_w, 'swa_out_w': swa_out_w, 'swa_q_norm': swa_q_norm, 'swa_k_norm': swa_k_norm,
        'swa_sinks': swa_sinks,
    }

def reference(x, mem, positions, norm_mix, norm_cross, norm_mem, norm_ffn,
              xq_w, xkv_w, xo_w, xq_norm, xk_norm,
              ffn_in_w, ffn_conv_w, ffn_conv_b, ffn_out_w,
              hyb_in_w, hyb_out_w, gdn_conv_w, gdn_a_log, gdn_dt_bias, gdn_norm,
              lru_conv_w, lru_conv_b, lru_wr, lru_br, lru_wi, lru_bi, lru_lambda,
              swa_in_w, swa_out_w, swa_q_norm, swa_k_norm, swa_sinks):
    cos, sin = rope_tables(positions, SWA_HD)
    for l in range(DEPTH):
        h = rmsnorm(x, norm_mix[l])
        if l % 2 == 0:
            e = l // 2
            qkv, z, b_raw, a_raw, lx, lg = split_cols(h @ hyb_in_w[e], HYB_SIZES)
            oa = gdn_mixer(qkv, z, b_raw, a_raw, gdn_conv_w[e], gdn_a_log[e], gdn_dt_bias[e], gdn_norm[e])
            ob = rglru_mixer(lx, lg, lru_conv_w[e], lru_conv_b[e], lru_wr[e], lru_br[e],
                             lru_wi[e], lru_bi[e], lru_lambda[e])
            mix = jnp.concatenate([oa, ob], axis=-1) @ hyb_out_w[e]
        else:
            o = l // 2
            mix = swa_mixer(h @ swa_in_w[o], swa_q_norm[o], swa_k_norm[o], swa_sinks[o], cos, sin) @ swa_out_w[o]
        x = x + mix
        x = x + cross_attn(rmsnorm(x, norm_cross[l]), rmsnorm(mem, norm_mem[l]),
                           xq_w[l], xkv_w[l], xo_w[l], xq_norm[l], xk_norm[l])
        x = x + conv_ffn(rmsnorm(x, norm_ffn[l]), ffn_in_w[l], ffn_conv_w[l], ffn_conv_b[l], ffn_out_w[l])
    return x


_drawn_inputs = setup_inputs


def setup_inputs(seed=0):
    import zlib

    import numpy as np

    out = dict(_drawn_inputs(seed))
    spreads = {}
    factors = {'norm_mix': 3.152,
     'norm_cross': 8.0,
     'norm_mem': 8.0,
     'norm_ffn': 2.83,
     'xq_norm': 8.0,
     'xk_norm': 8.0,
     'ffn_conv_b': 4.232,
     'gdn_norm': 6.244,
     'lru_br': 8.0,
     'lru_bi': 8.0,
     'swa_q_norm': 8.0,
     'swa_k_norm': 8.0,
     'swa_sinks': 23.304}
    for name, (base, spread) in spreads.items():
        noise = np.random.default_rng([zlib.crc32(name.encode()), seed]).standard_normal(out[name].shape)
        drawn = base * np.exp(spread * noise) if base else spread * noise
        out[name] = jnp.asarray(drawn.astype(out[name].dtype))
    for name, factor in factors.items():
        out[name] = (out[name] * factor).astype(out[name].dtype)
    return out
```

```python
import math
from contextlib import ExitStack

import numpy as np

import concourse.bass as bass
from concourse import mybir

F32 = mybir.dt.float32
F32R = mybir.dt.float32r
I32 = mybir.dt.int32
ALU = mybir.AluOpType
ACT = mybir.ActivationFunctionType
AX = mybir.AxisListType

P = 128
TOK = 256
TT = TOK // P
D = 2048
KT = D // P
DEPTH = 2
EPS = 1e-6
HEADS = 8
DK = 128
CHUNK = 64
NCHUNK = TOK // CHUNK
CONV = 4
LRU_TILES = 8
SWA_HD = 64
SWA_HEADS = 32
SWA_KV = 8
X_HEADS = 4
X_HD = 128
F_FF = 5632
FT = F_FF // P
FFN_CHUNKS = (16, 16, 12)

NK = 4
COLS = 256
NRAW = 4
NSPLIT = 4
AHEAD = 3

PAIRS = HEADS // 2
PAIR_TICKS = 24

HYB = 0
MEM = [HYB + PAIRS * PAIR_TICKS, 0]
MIXOUT = [MEM[0] + 16, 0]
XQ = [MIXOUT[0] + 32, 0]
MEM[1] = XQ[0] + 8
XO = [MEM[1] + 16, 0]
FFN = [XO[0] + 8, 0]
FFN_PIECES = sum(2 * (c // 2) * 4 + 8 * (c // 4) for c in FFN_CHUNKS)
SWKV = FFN[0] + FFN_PIECES
SWQ = SWKV + 16
MIXOUT[1] = SWQ + 32
XQ[1] = MIXOUT[1] + 32
XO[1] = XQ[1] + 8
FFN[1] = XO[1] + 8
PIECES = FFN[1] + FFN_PIECES

EARLY = [(0, 0), (0, 1), (0, 2), (1, 0), (1, 1), (1, 2), (0, 3), (1, 3)]

H_PHASE = {"x": 0, "mem0": 1, "mix0": 2, "mem1": 3, "xo0": 4, "ffn0": 5, "mix1": 6, "xo1": 7}
S_PHASE = {"x": 0, "mem0": 1, "mix0": 2, "xo0": 3, "ffn0": 4, "mix1": 5, "xo1": 6}

N_MEM = [0, 4]
N_XQ = [2, 16]
N_ROPE = 6


def mix_order(layer, t):
    return EARLY[t] if layer and t < 8 else (t // 4, t % 4)

CONST = {}


def constants():
    blocks = []

    def put(name, a):
        CONST[name] = sum(b.shape[1] for b in blocks)
        blocks.append(np.asarray(a, np.float32))

    i = np.arange(P)
    row, col = i[:, None], i[None, :]
    same = row // CHUNK == col // CHUNK
    put("ident", np.eye(P))
    put("ones", np.ones((P, P)))
    put("tri", same & (row <= col))
    put("chunk", same)
    put("half", row // 64 == col // 64)
    for s in (1, 2, 4, 8, 16, 32):
        put(f"level{s}", (row // (2 * s) == col // (2 * s)) & (row % (2 * s) >= s) & (col % (2 * s) < s))
    put("level1T", (row % 2 == 0) & (col == row + 1))
    put("swap", row == (col + 64) % P)
    rot = np.zeros((P, P))
    for m in range(P):
        if m % 64 < 32:
            rot[m + 32, m] = -1.0
        else:
            rot[m - 32, m] = 1.0
    put("rot", rot)
    put("band", np.concatenate([np.where(col > row, 0.0, -1e30), np.where(col <= row, 0.0, -1e30)], 1))
    freq = (1.0 / (np.float32(10000.0) ** (np.arange(0, 64, 2, dtype=np.float32) / np.float32(64)))).astype(np.float32)
    put("freq", freq[i % 32][:, None])
    return np.concatenate(blocks, 1)


CONST_COLS = constants().shape[1]

PARAMS = [
    ("norm_mix", 2 * KT), ("norm_cross", 2 * KT), ("norm_mem", 2 * KT), ("norm_ffn", 2 * KT),
    ("gdn_conv_w", CONV * 24), ("lru_conv_w", CONV * 8), ("lru_conv_b", 8), ("lru_br", 8), ("lru_bi", 8),
    ("lru_lambda", 8), ("gdn_norm", 1), ("xq_norm", 2), ("xk_norm", 2),
    ("ffn_conv_w", 2 * 3 * FT), ("ffn_conv_b", 2 * FT), ("swa_q_norm", 1), ("swa_k_norm", 1),
]
PCOL = {}
for _name, _rows in PARAMS:
    PCOL[_name] = sum(r for _, r in PARAMS[:len(PCOL)])
PARAM_ROWS = sum(r for _, r in PARAMS)
PARAM_TILES = -(-PARAM_ROWS // P)


class Link:

    def __init__(self, eng, sem):
        self.eng, self.sem, self.count, self.loop = eng, sem, 0, 0

    def __call__(self, ins):
        self.count += 1
        ins.then_inc(self.sem, 1)
        self.eng.wait_ge(self.sem, self.count + self.loop)

    def start(self, i, per):
        self.first, self.per, self.loop = self.count, per, i * per

    def end(self, turns):
        assert self.count - self.first == self.per, (self.count - self.first, self.per)
        self.count, self.loop = self.first + turns * self.per, 0


def trunk(nc, a, out):
    ctx = ExitStack()
    with ctx:
        def sb(name, shape, dt=F32, scope=ctx):
            return scope.enter_context(nc.sbuf_tensor(name, shape, dt))

        def sem(name):
            return ctx.enter_context(nc.semaphore(name))

        raw = sb("w_raw", [P, NRAW, NK, COLS])
        whi = sb("w_hi", [P, NSPLIT, NK, COLS], F32R)
        wlo = sb("w_lo", [P, NSPLIT, NK, COLS], F32R)
        xT = sb("xT", [P, KT, TOK])
        hhi = sb("h_hi", [P, KT, TOK], F32R)
        hlo = sb("h_lo", [P, KT, TOK], F32R)
        ahi = sb("act_hi", [P, 16, TOK], F32R)
        alo = sb("act_lo", [P, 16, TOK], F32R)
        cst = sb("cst", [P, CONST_COLS])
        par = sb("par", [P, PARAM_ROWS])
        rstd = sb("rstd", [P, TOK])
        rtmp = sb("rtmp", [P, TOK])
        ldiv = sb("bias_consts", [P, 8])
        rstd_m = sb("rstd_mem", [P, TOK])
        kvm = sb("kv_mem", [P, 2048])
        stage = sb("stage", [P, 2, 512])
        small = sb("small", [P, 64])
        cols = sb("gdn_cols", [P, 6, 16])
        rowp = sb("gdn_rows", [P, 2, 8])
        lruc = sb("lru_cols", [P, 3, 8])

        def c_(name, n=P):
            return cst[:, CONST[name]:CONST[name] + n]

        def pcol(name, k):
            return par[:, PCOL[name] + k:PCOL[name] + k + 1]

        ident, ones = c_("ident"), c_("ones")
        wr = kvm[:, 0:1024].rearrange("p (b j) -> p b j", b=8)
        wi = kvm[:, 1024:2048].rearrange("p (b j) -> p b j", b=8)
        eps_col, lnq_col, lnhalf_col, one_col = (ldiv[:, k:k + 1] for k in range(4))

        prow = stage[:].rearrange("p a b -> p (a b)")[:, 0:PARAM_TILES * P].rearrange("p (t c) -> p t c", c=P)
        wba = stage[:].rearrange("p a b -> p (a b)")[:, PARAM_TILES * P:PARAM_TILES * P + KT * 16].rearrange("p (k c) -> p k c", c=16)
        wbah = sb("ba_hi", [P, KT, 16], F32R)
        wbal = sb("ba_lo", [P, KT, 16], F32R)
        ba = sb("ba", [P, TT, 16])
        lp = sb("log1p", [P, 6, 24])
        rtok = sb("rstd_tok", [P, TT])

        s0 = ExitStack()
        with s0:
            x_tok = sb("x_tok", [P, TT, D], scope=s0)
            sq0 = sb("sq0", [P, 2, 512], scope=s0)
        beta, gg, gc, bexp, kds = (small[:, 16 * k:16 * k + 16] for k in (0, 1, 2, 3, 3))
        s1 = ExitStack()
        with s1:
            pads = sb("conv_pads", [P, 2, 2, TOK + 3], scope=s1)
            qb = sb("q_buf", [P, 512], scope=s1)
            kb = sb("k_buf", [P, 512], scope=s1)
            vbuf = sb("v_buf", [P, 512], scope=s1)
            zs = sb("z_silu", [P, 512], scope=s1)
            W4 = sb("gdn_work", [P, 4, 512], scope=s1)
            kbe = sb("k_beta_exp", [P, 512], scope=s1)
            kdec = sb("k_dec", [P, 512], scope=s1)
            vb = sb("v_beta", [P, 512], scope=s1)
            LT = sb("LT", [P, 512], scope=s1)
            at = sb("attnT", [P, 512], scope=s1)
            qd = sb("q_dec", [P, 512], scope=s1)
            usb = sb("u", [P, 512], scope=s1)
            wsb = sb("wT", [P, 512], scope=s1)
            vnew = sb("v_new", [P, 256], scope=s1)
            St = sb("state", [P, 256], scope=s1)
            egl = sb("exp_gl", [P, 8], scope=s1)
            ro = sb("o_rstd", [P, 512], scope=s1)
            xc = sb("lru_x", [P, 512], scope=s1)
            rt = sb("lru_r", [P, 512], scope=s1)
            it = sb("lru_i", [P, 512], scope=s1)
            l2 = sb("lru_l2", [P, 512], scope=s1)
            l1, gl_, osq = vbuf[:], kb[:], usb[:]
            msq = [qb[:], W4[:, 3, :]]
        s2 = ExitStack()
        with s2:
            xsq = sb("x_sq", [P, 2, 512], scope=s2)
            kvm1 = sb("kv_mem1", [P, 2048], scope=s2)
            nraw = sb("norm_raw", [P, 512], scope=s2)
            nsq = sb("norm_sq", [P, 512], scope=s2)
            nr = sb("norm_r", [P, 512], scope=s2)
            s6 = ExitStack()
            with s6:
                xq = sb("xq", [P, X_HEADS, TOK], scope=s6)
                xp = sb("x_probs", [P, 2, 512], scope=s6)
                xpT = sb("x_probsT", [P, 2, 512], scope=s6)
                xmx = sb("x_max", [P, X_HEADS, 6], scope=s6)
            s3 = ExitStack()
            with s3:
                gpad = sb("ffn_pad", [P, 1, 2, TOK + 2], scope=s3)
                gcv = sb("ffn_conv", [P, 1, 512], scope=s3)
                fup = sb("ffn_up", [P, 512], scope=s3)
            s4 = ExitStack()
            with s4:
                posi = sb("pos_int", [P, TOK], I32, scope=s4)
                cosb = sb("cos", [P, TOK], scope=s4)
                sinb = sb("sin", [P, TOK], scope=s4)
                ang = sb("angle", [P, 3, TOK], scope=s4)
                kTt = sb("kT", [P, 4, TOK], scope=s4)
                kTs = sb("kT_swapped", [P, 4, TOK], scope=s4)
                vtok = sb("v_tok", [P, TT, 4, P], scope=s4)
                qf = sb("q_rot", [P, 512], scope=s4)
                sc = sb("scores", [P, 4, 384], scope=s4)
                pT = sb("probsT", [P, 12, P], scope=s4)
                sst = sb("softmax_small", [P, 6, 8], scope=s4)
                sinks = sb("sinks", [P, SWA_HEADS], scope=s4)
            s5 = ExitStack()
            with s5:
                ost = sb("out_stage", [P, 2, TT, 256], scope=s5)

        xk = [m[:, 0:1024].rearrange("p (h m) -> p h m", h=X_HEADS) for m in (kvm, kvm1)]
        xv = [m[:, 1024:2048].rearrange("p (t h d) -> p t h d", t=TT, h=X_HEADS) for m in (kvm, kvm1)]

        ST = [ctx.enter_context(nc.psum_tensor(f"stream{i}", [P, 512], F32)) for i in range(2)]
        B = [ctx.enter_context(nc.psum_tensor(f"bank{i}", [P, 512], F32)) for i in range(6)]

        w_loaded = [sem(f"w_loaded{i}") for i in range(NRAW)]
        hi_split, lo_split = sem("hi_split"), sem("lo_split")
        pieces_done, group_evac = sem("pieces_done"), sem("group_evac")
        dve_link, act_link = sem("dve_link"), sem("act_link")
        x_loaded, c_loaded, p_loaded, b_loaded = sem("x_loaded"), sem("c_loaded"), sem("p_loaded"), sem("b_loaded")
        gain_loaded = sem("gain_rows_loaded")
        ba_loaded, consts_set, rstd_guess = sem("ba_loaded"), sem("consts_set"), sem("rstd_guess")
        prowT, par_ready = sem("param_rows_transposed"), sem("par_ready")
        xtT, xt_copied, sq_ready = sem("x_transposed"), sem("xT_copied"), sem("square_ready")
        ss_done, rstd_ready, h_ready = sem("sumsq_done"), sem("rstd_ready"), sem("h_ready")
        rtok_ready = sem("rstd_tok_ready")
        ba_split, ba_done = sem("ba_split"), sem("ba_done")
        ln_in, ln_out, g_ready, gc_done, cols_in, cols_out = (sem(n) for n in (
            "gates_in", "gates_exp", "g_ready", "gc_done", "gate_cols_in", "gate_cols_exp"))
        conv_done, silu_done = sem("conv_done"), sem("silu_done")
        qk_sq, qk_ss, qk_r, qk_n = sem("qk_squared"), sem("qk_sumsq"), sem("qk_rstd"), sem("qk_normed")
        gram_done, dmin, dexp, lt_ready = sem("gram_done"), sem("decay_arg"), sem("decay_exp"), sem("LT_ready")
        kt_scaled, vT_done, vb_ready = sem("k_scaled"), sem("v_transposed"), sem("v_beta_ready")
        lx_done, x_masked, tu_done, tu_ready = sem("LX_done"), sem("X_masked"), sem("TU_done"), sem("TU_ready")
        uw_done, u_ready, w_ready = sem("uw_done"), sem("u_ready"), sem("w_ready")
        ws_done, vn_ready, os_done, s_ready = sem("wS_done"), sem("v_new_ready"), sem("oS_done"), sem("state_ready")
        o_sq, o_ss, o_r, gdn_out = sem("o_squared"), sem("o_sumsq"), sem("o_rstd_ready"), sem("gdn_out")
        z_ready = sem("z_ready")
        xc_ready, ri_done, ri_tanh, la_ready = sem("lru_x_ready"), sem("lru_ri_done"), sem("lru_ri_tanh"), sem("lru_la_ready")
        lru_ln, lru_dif, lru_root, gate_in, gate_out, lru_out = (sem(n) for n in (
            "lru_logs", "lru_log_ratio", "lru_root", "lru_gate_in", "lru_gate_gelu", "lru_out"))
        m_loaded, mT_done, m_split = sem("mem_loaded"), sem("mem_transposed"), sem("mem_split")
        n_raw, n_sq, n_ss, n_r, n_out = (sem(n) for n in ("head_raw", "head_squared", "head_sumsq", "head_rstd", "head_normed"))
        xvr, xvT, xv_ready = sem("mem_v_raw"), sem("mem_v_transposed"), sem("mem_v_ready")
        xs_done, xneg, xexp, xpn, xpt_done, xpt_copied, xo_done, xo_out = (sem(n) for n in (
            "x_scores", "x_negmax", "x_exp", "x_probs_ready", "x_probsT_done", "x_probsT_copied", "x_pv_done", "x_out"))
        x_new = sem("x_updated")
        gt_conv, gt_silu, ffn_act = sem("ffn_conv_done"), sem("ffn_silu"), sem("ffn_act")
        pos_loaded, ang_ready, trig_ready = sem("pos_loaded"), sem("angles"), sem("trig")
        rot_done, kT_done, ksw_done, ksw_ready = sem("rot_done"), sem("kT_ready"), sem("k_swap_done"), sem("k_swap_ready")
        q_rot, sv_raw, svT, sv_ready = sem("q_rotated"), sem("swa_v_raw"), sem("swa_v_transposed"), sem("swa_v_ready")
        even_heads = sem("even_heads_scores")
        s_done, s_masked, s_neg, s_exp, s_prob = (sem(n) for n in (
            "scores_done", "scores_masked", "scores_negmax", "scores_exp", "probs_ready"))
        pt_done, pt_copied, pv_done, swa_out = sem("probsT_done"), sem("probsT_copied"), sem("pv_done"), sem("swa_out")
        oT_done, o_staged, o_stored = sem("out_transposed"), sem("out_staged"), [sem(f"out_stored{i}") for i in range(2)]

        def stage_groups():
            first, g = {}, 0
            for start, groups in ([(HYB, 24), (MEM[0], 4), (MIXOUT[0], 8), (XQ[0], 2), (MEM[1], 4), (XO[0], 8), (FFN[0], 0)]
                                  + [(SWKV, 4), (SWQ, 8), (MIXOUT[1], 8), (XQ[1], 2), (XO[1], 8), (FFN[1], 0)]):
                first[start] = g
                g += groups or sum(c + 8 for c in FFN_CHUNKS)
            return first

        GROUP = stage_groups()

        def ffn_parts(layer):
            n, g, tile = FFN[layer], GROUP[FFN[layer]], 0
            for c, size in enumerate(FFN_CHUNKS):
                yield c, size, tile, n, g
                n += size * 4 + 2 * size
                g += size + 8
                tile += size

        block = ctx.enter_context(nc.Block())

        @block.sync
        def _(sp):
            xv_ = a["x"].rearrange("b (t p) d -> p (b t) d", p=P)
            for t in range(TT):
                sp.dma_start(x_tok[:, t, :], xv_[:, t, :]).then_inc(x_loaded, 16)
            sp.dma_start(cst[:], a["consts"]).then_inc(c_loaded, 16)

            def load(n, k, turn, src, rows, c0):
                if not isinstance(n, int) or n >= NRAW:
                    sp.wait_ge(lo_split, n - NRAW + 1)
                sp.dma_start(raw[:, k], src[rows:rows + NK * P, bass.ds(c0, COLS)]
                             .rearrange("(k p) c -> p k c", p=P)).then_inc(w_loaded[k], 16)

            def load_group(n, src, c0, quarters=4):
                for q in range(quarters):
                    load(n + q, (n + q) % NRAW, 0, src, q * NK * P, c0)

            hyb = a["hyb_in_w"][0]
            starts = [0, 1024, 2048, 3072, 4112, 5136]
            for p in range(PAIRS):
                for j, s in enumerate(starts):
                    load_group(HYB + p * PAIR_TICKS + 4 * j, hyb, s + p * COLS)

            def load_mem(layer):
                for g in range(4):
                    load_group(MEM[layer] + 4 * g, a["xkv_w"][layer], g * COLS)

            def load_common(layer, mixout):
                for t in range(32):
                    g, q = mix_order(layer, t)
                    load(MIXOUT[layer] + t, t % NRAW, 0, mixout, q * NK * P, g * COLS)
                for g in range(2):
                    load_group(XQ[layer] + 4 * g, a["xq_w"][layer], g * COLS)
                if layer == 0:
                    load_mem(1)
                for g in range(8):
                    load(XO[layer] + g, g % NRAW, 0, a["xo_w"][layer], 0, g * COLS)
                for c, size, tile, n, g in ffn_parts(layer):
                    with sp.Fori(0, size // 2) as i:
                        for half in range(2):
                            for q in range(4):
                                load(n + 4 * half + q + i * 8, q, 0, a["ffn_in_w"][layer], q * NK * P,
                                     half * F_FF + tile * P + i * COLS)
                    n += 4 * size
                    quarters = size // 4
                    for g in range(8):
                        for q in range(quarters):
                            load(n + g * quarters + q, (g * quarters + q) % NRAW, 0, a["ffn_out_w"][layer],
                                 (tile + 4 * q) * P, g * COLS)

            load_mem(0)
            load_common(0, a["hyb_out_w"][0])
            for g in range(4):
                load_group(SWKV + 4 * g, a["swa_in_w"][0], SWA_HEADS * SWA_HD + g * COLS)
            for g in range(8):
                load_group(SWQ + 4 * g, a["swa_in_w"][0], g * COLS)
            load_common(1, a["swa_out_w"][0])
            for s in o_stored:
                sp.wait_ge(s, 16 * 4)

        @block.gpsimd
        def _(pool):
            pool.dma_start(rowp[:, 0, :], a["gdn_a_log"].rearrange("a h -> (a h)").partition_broadcast(P)).then_inc(b_loaded, 16)
            pool.dma_start(rowp[:, 1, :], a["gdn_dt_bias"].rearrange("a h -> (a h)").partition_broadcast(P)).then_inc(b_loaded, 16)
            pool.dma_start(wr, a["lru_wr"].rearrange("a b i j -> i (a b) j")).then_inc(b_loaded, 16)
            pool.dma_start(wi, a["lru_wi"].rearrange("a b i j -> i (a b) j")).then_inc(b_loaded, 16)
            pool.wait_ge(prowT, PARAM_TILES)
            pool.wait_ge(ba_split, 1)

            def load_mem(layer):
                mv = a["mem"].rearrange("b (t p) d -> p (b t) d", p=P)
                for j in range(4):
                    if layer or j:
                        pool.wait_ge(mT_done, 4 * layer + j)
                    pool.dma_start(stage[:], mv[:, :, 512 * j:512 * j + 512]).then_inc(m_loaded, 16)

            load_mem(0)
            load_mem(1)
            pool.wait_ge(pieces_done, SWKV)
            pool.dma_start(posi[:], a["positions"].rearrange("b s -> (b s)").partition_broadcast(P)).then_inc(pos_loaded, 16)
            pool.dma_start(sinks[:], a["swa_sinks"].rearrange("a h -> (a h)").partition_broadcast(P)).then_inc(pos_loaded, 16)

        GAIN_DMAS = 4
        P_DMAS = sum(len(range(PCOL[n] // P, (PCOL[n] + r - 1) // P + 1)) for n, r in PARAMS) + 2 - GAIN_DMAS

        @block.scalar
        def _(act):
            link = Link(act, act_link)
            f = nc.scalar.activation

            def split(n, i=0):
                if n >= PIECES:
                    return
                k = n % NSPLIT
                act.wait_ge(w_loaded[n % NRAW], 16 * (n // NRAW + 1) + 16 * (8 // NRAW) * i)
                if n >= NSPLIT:
                    act.wait_ge(pieces_done, n - NSPLIT + 1 + 8 * i)
                nc.scalar.copy(whi[:, k], raw[:, n % NRAW]).then_inc(hi_split, 1)

            def tables(name):
                nc.scalar.preload_act_table_set(name)

            LN_EXP, SILU, GELU = "natural_log_exp_and_others", "silu_and_others", "gelu_apprx_tanh_and_others"

            def square(phase, g, src, dst):
                count = 8 * phase + g
                if g >= 2:
                    act.wait_ge(ss_done, count - 1)
                f(dst, src, ACT.Square).then_inc(sq_ready, 1)

            def row_rstd(phase):
                act.wait_ge(ss_done, 8 * phase + 8)
                tables(LN_EXP)
                link(f(rtmp[:], B[5 if phase == S_PHASE["mem0"] else 0][:, 0:TOK], ACT.Ln, bias=eps_col, scale=1.0 / D))
                f((rstd_m if phase == S_PHASE["mem0"] else rstd)[:], rtmp[:], ACT.Exp, scale=-0.5).then_inc(rstd_guess, 1)

            for name, rows in PARAMS:
                v = a[name]
                if name in ("swa_q_norm", "swa_k_norm"):
                    r = PCOL[name]
                    for h in range(2):
                        act.dma_start(prow[r % P:r % P + 1, r // P, 64 * h:64 * h + 64], v).then_inc(p_loaded, 16)
                    continue
                flat = v.rearrange({2: "a b -> (a b)", 3: "a b c -> (a b c)"}[len(v.shape)]).rearrange("(r c) -> r c", c=P)
                done = 0
                while done < rows:
                    r = PCOL[name] + done
                    n = min(rows - done, P - r % P)
                    act.dma_start(prow[r % P:r % P + n, r // P, :], flat[done:done + n, :]).then_inc(
                        gain_loaded if r < P else p_loaded, 16)
                    done += n
            act.dma_start(wba[:], a["hyb_in_w"][0, :, 4096:4112].rearrange("(k p) c -> p k c", p=P)).then_inc(ba_loaded, 16)
            act.wait_ge(consts_set, 1)
            for g in range(8):
                act.wait_ge(xt_copied, g + 1)
                square(0, g, xT[:, 2 * g:2 * g + 2, :], sq0[:, g % 2])
                if g in (1, 3, 5):
                    split(g // 2)
            row_rstd(0)

            def gates(t):
                if t == 2:
                    act.wait_ge(b_loaded, 64)
                    f(cols[:, 5, 0:8], rowp[:, 0, :], ACT.Exp).then_inc(ln_out, 1)
                    act.wait_ge(ln_in, 1)
                    f(lp[:, 1, :], lp[:, 0, :], ACT.Exp).then_inc(ln_out, 1)
                    f(cols[:, 4, :], cols[:, 0, :], ACT.Exp, scale=-1.0).then_inc(ln_out, 1)
                if t == 7:
                    tables(LN_EXP)
                    act.wait_ge(cols_in, 1)
                    f(cols[:, 3, :], cols[:, 2, :], ACT.Exp).then_inc(cols_out, 1)
                    f(cols[:, 4, :], cols[:, 1, :], ACT.Exp).then_inc(cols_out, 1)

            def head_square(ni, g, src, dst):
                act.wait_ge(group_evac, g + 1)
                if ni:
                    act.wait_ge(n_ss, ni)
                f(dst, src, ACT.Square).then_inc(n_sq, 1)

            def head_rstd(ni, bank, dst, width):
                act.wait_ge(n_ss, ni + 1)
                if ni:
                    act.wait_ge(n_out, ni)
                tables(LN_EXP)
                link(f(dst, bank, ACT.Ln, bias=eps_col, scale=1.0 / width))
                f(dst, dst, ACT.Exp, scale=-0.5).then_inc(n_r, 1)

            def scale_keys(p):
                act.wait_ge(gram_done, p + 1)
                for u in range(4):
                    h, tt = 2 * p + u // 2, u % TT
                    s = slice(u * P, u * P + P)
                    nc.scalar.activation(kbe[:, s], B[0][:, s], ACT.Copy, scale=bexp[:, tt * 8 + h:tt * 8 + h + 1])
                    last = nc.scalar.activation(kdec[:, s], B[0][:, s], ACT.Copy,
                                                scale=cols[:, 3, tt * 8 + h:tt * 8 + h + 1])
                last.then_inc(kt_scaled, 1)

            def gdn_front(p, t):
                if t == 8:
                    act.wait_ge(silu_done, 3 * p + 2)
                    if p:
                        act.wait_ge(uw_done, p)
                    f(W4[:, 0, :], qb[:], ACT.Square).then_inc(qk_sq, 1)
                    f(W4[:, 1, :], kb[:], ACT.Square).then_inc(qk_sq, 1)
                if t == 9:
                    act.wait_ge(qk_ss, p + 1)
                    tables(LN_EXP)
                    f(W4[:, 2, :], B[0][:], ACT.Ln, bias=eps_col)
                    link(f(W4[:, 3, :], B[1][:], ACT.Ln, bias=eps_col))
                    f(W4[:, 2, :], W4[:, 2, :], ACT.Exp, scale=-0.5, bias=lnq_col).then_inc(qk_r, 1)
                    f(W4[:, 3, :], W4[:, 3, :], ACT.Exp, scale=-0.5).then_inc(qk_r, 1)
                if t == 11:
                    act.wait_ge(dmin, p + 1)
                    f(W4[:, 3, :], W4[:, 3, :], ACT.Exp).then_inc(dexp, 1)
                    f(vb[:], B[1][:], ACT.Exp).then_inc(dexp, 1)
                    f(egl[:], B[1][:, CHUNK - 1::CHUNK], ACT.Exp).then_inc(dexp, 1)
                if t == 12:
                    scale_keys(p)
                if t in (3, 7, 13):
                    j = t // 4 if t < 12 else 2
                    buf = (qb, kb, vbuf)[j]
                    if j != 1 or p == 0:
                        tables(SILU)
                    act.wait_ge(conv_done, 3 * p + j + 1)
                    f(buf[:], buf[:], ACT.Silu).then_inc(silu_done, 1)
                if t == 15:
                    act.wait_ge(vT_done, p + 1)
                    act.wait_ge(lt_ready, p + 1)
                    for u in range(4):
                        h, tt = 2 * p + u // 2, u % TT
                        s = slice(u * P, u * P + P)
                        last = nc.scalar.activation(vb[:, s], B[1][:, s], ACT.Copy, scale=beta[:, tt * 8 + h:tt * 8 + h + 1])
                    last.then_inc(vb_ready, 1)
                if t == 15:
                    act.wait_ge(group_evac, 6 * p + 4)
                    f(zs[:], zs[:], ACT.Silu).then_inc(z_ready, 1)
                if t == 20:
                    act.wait_ge(ri_done, p + 1)
                    if p:
                        act.wait_ge(lru_out, p)
                    tables(GELU)
                    for b in range(2):
                        s = slice(b * TOK, b * TOK + TOK)
                        k = 2 * p + b
                        f(rt[:, s], B[0][:, s], ACT.Tanh, scale=0.5, bias=lruc[:, 0, k:k + 1])
                        last = f(it[:, s], B[1][:, s], ACT.Tanh, scale=0.5, bias=lruc[:, 1, k:k + 1])
                    last.then_inc(ri_tanh, 1)
                if t == 21:
                    act.wait_ge(la_ready, p + 1)
                    f(l2[:], rt[:], ACT.Tanh, scale=-1.0).then_inc(lru_ln, 1)
                if t == 23:
                    act.wait_ge(group_evac, 6 * p + 6)
                    f(gl_, gl_, ACT.Gelu_apprx_tanh).then_inc(gate_out, 1)

            def gdn_tail(p, t):
                if t == 0:
                    act.wait_ge(uw_done, p + 1)
                    if p:
                        act.wait_ge(ws_done, 3 * p)
                    nc.scalar.copy(wsb[:], B[3][:]).then_inc(w_ready, 1)
                    tables(LN_EXP)
                    act.wait_ge(lru_ln, 4 * p + 1)
                    f(rt[:], rt[:], ACT.Exp).then_inc(lru_ln, 1)
                    f(l1, l2[:], ACT.Ln, bias=one_col).then_inc(lru_ln, 1)
                    f(l2[:], l2[:], ACT.Ln, scale=2.0, bias=ldiv[:, 4:5]).then_inc(lru_ln, 1)
                if t == 1:
                    act.wait_ge(lru_dif, p + 1)
                    f(l2[:], l2[:], ACT.Exp, scale=0.5, bias=lnhalf_col).then_inc(lru_root, 1)
                if t == 7:
                    act.wait_ge(os_done, 4 * p + 4)
                    f(osq, B[5][:], ACT.Square).then_inc(o_sq, 1)
                if t == 8:
                    act.wait_ge(o_ss, p + 1)
                    tables(LN_EXP)
                    link(f(ro[:], B[4][:], ACT.Ln, bias=eps_col, scale=1.0 / DK))
                    f(ro[:], ro[:], ACT.Exp, scale=-0.5).then_inc(o_r, 1)


            def mem_quarter(layer, j):
                if layer == 0:
                    for g in (2 * j, 2 * j + 1):
                        act.wait_ge(mT_done, j + 1)
                        if g == 0:
                            act.wait_ge(xtT, 8)
                        square(S_PHASE["mem0"], g, B[g % 2][:], msq[g % 2])

            def mem_side(layer, t):
                n0, s, r = ((qb, kb, vbuf) if layer == 0 else (nraw, nsq, nr))
                g = t // 4
                if t in (3, 7):
                    head_square(N_MEM[layer] + g, GROUP[MEM[layer]] + g, n0[:], s[:])
                if t in (4, 8):
                    head_rstd(N_MEM[layer] + g - 1, B[0][:], r[:], X_HD)
                if t in (12, 16):
                    act.wait_ge(xvT, 2 * layer + g - 2)
                    nc.scalar.copy(xv[layer][:, :, 2 * (g - 3):2 * (g - 3) + 2, :],
                                   B[1][:].rearrange("p (t h d) -> p t h d", t=TT, h=2)).then_inc(xv_ready, 1)

            for p in range(PAIRS):
                for t in range(PAIR_TICKS):
                    split(HYB + PAIR_TICKS * p + t + AHEAD)
                    gdn_front(p, t)
                    if p:
                        gdn_tail(p - 1, t)
                    else:
                        gates(t)
                    if p == PAIRS - 1 and t >= 21:
                        mem_quarter(0, t - 21)

            def residual(phase, start, g, ticks):
                act.wait_ge(group_evac, GROUP[start] + g + 1)
                square(phase, g, xT[:, 2 * g:2 * g + 2, :], xsq[:, g % 2])

            def cross(layer):
                def exps(h):
                    act.wait_ge(xneg, 4 * layer + h + 1)
                    for u in range(2):
                        last = f(xp[:, h % 2, u * TOK:u * TOK + TOK], B[2 + h % 2][:, u * TOK:u * TOK + TOK], ACT.Exp,
                                 scale=X_HD ** -0.5, bias=xmx[:, h, 2 + u:3 + u], accum_out=xmx[:, h, 4 + u:5 + u])
                    last.then_inc(xexp, 1)

                def copy(h):
                    act.wait_ge(xpt_done, 4 * layer + h + 1)
                    if h >= 2:
                        act.wait_ge(xo_done, 4 * layer + h - 1)
                    nc.scalar.copy(xpT[:, h % 2], B[4][:]).then_inc(xpt_copied, 1)

                return exps, copy

            def common(layer):
                def mixout(t):
                    split(MIXOUT[layer] + t + AHEAD)
                    g, q = mix_order(layer, t)
                    if q == 3:
                        residual(S_PHASE[f"mix{layer}"], MIXOUT[layer], g, 4)

                first = 0
                if layer == 1:
                    for t in range(32, 41):
                        if t < 38:
                            mixout(t - 32)
                        swa_first(t)
                        swa_side(t)
                    first = 6
                for t in range(first, 32):
                    mixout(t)
                    if t == 0:
                        mem_side(0, 16)
                row_rstd(S_PHASE[f"mix{layer}"])
                ni = N_XQ[layer]
                HB = B[1 if layer else 5]
                exps, copy = cross(layer)
                for t in range(8):
                    split(XQ[layer] + t + AHEAD)
                    if layer and t == 6:
                        exps(0)
                        exps(1)
                    if t in (3, 7):
                        head_square(ni + t // 4, GROUP[XQ[layer]] + t // 4, nraw[:], nsq[:])
                    if t == 4:
                        head_rstd(ni, HB[:], nr[:], X_HD)
                    if layer and t == 7:
                        copy(0)
                if layer == 0:
                    for t in range(16):
                        split(MEM[1] + t + AHEAD)
                        if t == 0:
                            head_rstd(ni + 1, HB[:], nr[:], X_HD)
                        if t == 2:
                            exps(0)
                            exps(1)
                        if t in (3, 5, 7, 9):
                            copy((t - 3) // 2)
                        if t in (4, 6):
                            exps(t // 2)
                        mem_side(1, t)
                else:
                    head_rstd(ni + 1, HB[:], nr[:], X_HD)
                    copy(1)
                    exps(2)
                    exps(3)
                    copy(2)
                    copy(3)
                for g in range(8):
                    split(XO[layer] + g + AHEAD)
                    if layer == 0 and g == 0:
                        mem_side(1, 16)
                    residual(S_PHASE[f"xo{layer}"], XO[layer], g, 1)
                row_rstd(S_PHASE[f"xo{layer}"])
                tables(SILU)
                for c, size, tile, n, g0 in ffn_parts(layer):
                    done = (tile // 2) + layer * (FT // 2)
                    with act.Fori(0, size // 2) as i:
                        for t in range(8):
                            split(n + t + AHEAD, i)
                            if t == 3:
                                act.wait_ge(gt_conv, done + 1 + i)
                                f(gcv[:, 0], gcv[:, 0], ACT.Silu).then_inc(gt_silu, 1)
                    n += 4 * size
                    g0 += size
                    q = size // 4
                    for g in range(8):
                        for t in range(q):
                            split(n + g * q + t + AHEAD)
                            if c == 2 and layer == 1 and g and t == 1:
                                store(g - 1)
                        if c == 2 and layer == 0:
                            act.wait_ge(group_evac, g0 + g + 1)
                            square(S_PHASE["ffn0"], g, xT[:, 2 * g:2 * g + 2, :], xsq[:, g % 2])

            def store(g):
                act.wait_ge(oT_done, g + 1)
                if g >= 2:
                    act.wait_ge(o_stored[g % 2], 16 * (g // 2))
                nc.scalar.copy(ost[:, g % 2].rearrange("p t (k c) -> p k t c", k=2),
                               B[1 + g % 2][:].rearrange("p (k t c) -> p k t c", k=2, t=TT)).then_inc(o_staged, 1)
                act.wait_ge(o_staged, g + 1)
                act.dma_start(out.rearrange("b (t p) d -> p (b t) d", p=P)[:, :, g * COLS:(g + 1) * COLS],
                              ost[:, g % 2]).then_inc(o_stored[g % 2], 16)

            def swa_rope(ni, g, t):
                if t == 3:
                    head_square(ni, g, nraw[:], nsq[:])
                if t == 4:
                    head_rstd(ni, B[0][:], nr[:], SWA_HD)

            def swa_first(t):
                g = (t - 8) // 4
                if 8 <= t and g < 8 and t == 4 * g + 8:
                    act.wait_ge(s_neg, g + 1)
                    for i in range(4):
                        f(sc[:, i, 0:P], sc[:, i, 0:P], ACT.Exp, bias=sst[:, 1, i:i + 1], accum_out=sst[:, 2, i:i + 1])
                        f(sc[:, i, P:384], sc[:, i, P:384], ACT.Exp, bias=sst[:, 1, 4 + i:5 + i], accum_out=sst[:, 2, 4 + i:5 + i])
                    f(sst[:, 4, :], sst[:, 3, :], ACT.Exp).then_inc(s_exp, 1)

            def swa_side(t):
                g = (t - 3) // 4
                if 3 <= t and g < 8 and t - 4 * g == 3:
                    swa_rope(N_ROPE + 2 + g, GROUP[SWQ] + g, 3)
                g = (t - 4) // 4
                if 4 <= t and g < 8 and t == 4 * g + 4:
                    swa_rope(N_ROPE + 2 + g, 0, 4)
                g = (t - 10) // 4
                if 10 <= t and g < 8 and t == 4 * g + 10:
                    act.wait_ge(pt_done, g + 1)
                    if g:
                        act.wait_ge(pv_done, g)
                    for b in range(3):
                        last = nc.scalar.copy(pT[:, 4 * b:4 * b + 4, :], B[2 + b][:].rearrange("p (k c) -> p k c", k=4))
                    last.then_inc(pt_copied, 1)

            for t in range(16):
                split(MEM[0] + t + AHEAD)
                gdn_tail(PAIRS - 1, t)
                if t == 0:
                    mem_quarter(0, 3)
                if t == 1:
                    row_rstd(S_PHASE["mem0"])
                mem_side(0, t)
            common(0)
            row_rstd(S_PHASE["ffn0"])
            act.wait_ge(ang_ready, 1)
            tables(SILU)
            f(sinb[:], ang[:, 0, :], ACT.Sin).then_inc(trig_ready, 1)
            f(cosb[:], ang[:, 1, :], ACT.Sin).then_inc(trig_ready, 1)
            for t in range(16):
                split(SWKV + t + AHEAD)
                g, k = t // 4, t % 4
                if g < 2 and k == 3:
                    swa_rope(N_ROPE + g, GROUP[SWKV] + g, 3)
                if t in (4, 8):
                    swa_rope(N_ROPE + g - 1, 0, 4)
                if t in (7, 11):
                    act.wait_ge(ksw_done, g)
                    nc.scalar.copy(kTs[:, 2 * (g - 1):2 * g, :], B[2][:].rearrange("p (k c) -> p k c", k=2)).then_inc(ksw_ready, 1)
                if t == 12:
                    act.wait_ge(svT, 1)
                    nc.scalar.copy(vtok[:, :, 0:2, :], B[0][:].rearrange("p (t k c) -> p t k c", t=TT, k=2)).then_inc(sv_ready, 1)
            for t in range(32):
                split(SWQ + t + AHEAD)
                swa_first(t)
                if t == 0:
                    act.wait_ge(svT, 2)
                    nc.scalar.copy(vtok[:, :, 2:4, :], B[0][:].rearrange("p (t k c) -> p t k c", t=TT, k=2)).then_inc(sv_ready, 1)
                swa_side(t)
            common(1)
            store(7)

        @block.vector
        def _(dve):
            link = Link(dve, dve_link)
            v = nc.vector

            def split(n, i=0):
                if n >= PIECES:
                    return
                k = n % NSPLIT
                dve.wait_ge(hi_split, n + 1 + 8 * i)
                v.tensor_tensor(wlo[:, k], raw[:, n % NRAW], whi[:, k].bitcast(F32), ALU.subtract).then_inc(lo_split, 1)

            def two(ap):
                return ap.rearrange("p (k c) -> p k c", k=2)

            def evac_scaled(dst, start, gi, n, i=0, rows=rstd):
                dve.wait_ge(pieces_done, n + 1 + 8 * i)
                r = rows[:].unsqueeze(1).to_broadcast([P, 2, TOK])
                v.tensor_tensor(dst, two(ST[gi % 2][:]), r, ALU.mult).then_inc(group_evac, 1)

            def refine(r, u, total, width):
                link(v.scalar_tensor_tensor(u, total, EPS * width, r, ALU.add, ALU.mult))
                link(v.scalar_tensor_tensor(u, u, -0.5 / width, r, ALU.mult, ALU.mult))
                return v.scalar_tensor_tensor(r, u, 1.5, r, ALU.add, ALU.mult)

            def refine_rows(phase):
                dve.wait_ge(rstd_guess, phase + 1)
                mem = phase == S_PHASE["mem0"]
                refine((rstd_m if mem else rstd)[:], rtmp[:], B[5 if mem else 0][:, 0:TOK], D).then_inc(rstd_ready, 1)
                dve.wait_ge(rstd_ready, phase + 1)

            def split_act(dst, src, done):
                link(v.tensor_copy(ahi[:, dst, :], src))
                v.tensor_tensor(alo[:, dst, :], src, ahi[:, dst, :].bitcast(F32), ALU.subtract).then_inc(done, 1)

            def split_h(g, src, gain, k):
                for b in range(2):
                    s = src[:, b * TOK:b * TOK + TOK]
                    last = v.tensor_scalar(hhi[:, 2 * g + b, :], s, pcol(gain, k + 2 * g + b), None, ALU.mult)
                link(last)
                for b in range(2):
                    s = src[:, b * TOK:b * TOK + TOK]
                    last = v.scalar_tensor_tensor(hlo[:, 2 * g + b, :], s, pcol(gain, k + 2 * g + b),
                                                  hhi[:, 2 * g + b, :].bitcast(F32), ALU.mult, ALU.subtract)
                last.then_inc(h_ready, 1)

            def conv(pad, dst, name, col, stride, taps, bias=None):
                for b in range(2):
                    if bias is None:
                        last = v.tensor_scalar(dst[:, b * TOK:b * TOK + TOK], pad[:, b, taps - 1:taps - 1 + TOK],
                                               par[:, col(taps - 1, b)], None, ALU.mult)
                    else:
                        last = v.tensor_scalar(dst[:, b * TOK:b * TOK + TOK], pad[:, b, taps - 1:taps - 1 + TOK],
                                               par[:, col(taps - 1, b)], par[:, bias(b)], ALU.mult, ALU.add)
                for j in range(taps - 1):
                    link(last)
                    for b in range(2):
                        d = dst[:, b * TOK:b * TOK + TOK]
                        last = v.scalar_tensor_tensor(d, pad[:, b, j:j + TOK], par[:, col(j, b)], d, ALU.mult, ALU.add)
                return last

            for k, value in enumerate((EPS, math.log(DK ** -0.5), math.log(0.5), 1.0, 1e-18)):
                last = v.memset(ldiv[:, k:k + 1], value)
            last.then_inc(consts_set, 1)
            def param_tile(j):
                n = min(P, PARAM_ROWS - j * P)
                dve.wait_ge(prowT, j + 1)
                v.tensor_copy(par[:, j * P:j * P + n], B[3 + j % 2][:, 0:n]).then_inc(par_ready, 1)
                dve.wait_ge(par_ready, j + 1)

            param_tile(0)
            for g in range(8):
                dve.wait_ge(xtT, g + 1)
                v.tensor_copy(xT[:, 2 * g:2 * g + 2, :], two(B[1 + g % 2][:])).then_inc(xt_copied, 1)
                dve.wait_ge(xt_copied, g + 1)
                split_h(g, xT[:, 2 * g:2 * g + 2, :].rearrange("p k c -> p (k c)"), "norm_mix", 0)
                if g in (1, 3, 5):
                    split(g // 2)
            link(v.memset(pads[:, :, :, 0:CONV - 1], 0.0))
            c3 = lambda ap: ap.rearrange("p (t h) -> p t h", t=TT)

            def gates(t):
                if t == 0:
                    for j in range(1, PARAM_TILES):
                        param_tile(j)
                    refine_rows(S_PHASE["x"])
                if t == 1:
                    dve.wait_ge(ba_loaded, 16)
                    link(v.tensor_copy(wbah[:], wba[:]))
                    v.tensor_tensor(wbal[:], wba[:], wbah[:].bitcast(F32), ALU.subtract).then_inc(ba_split, 1)
                if t == 2:
                    dve.wait_ge(b_loaded, 64)
                    dve.wait_ge(rtok_ready, 1)
                    for t in range(TT):
                        last = v.tensor_copy(rtok[:, t:t + 1], B[4][:, t * P:t * P + 1])
                    link(last)
                    dve.wait_ge(ba_done, 1)
                    for t in range(TT):
                        last = v.tensor_scalar(ba[:, t, :], B[3][:, t * 16:t * 16 + 16], rtok[:, t:t + 1], None, ALU.mult)
                    link(last)
                    link(v.tensor_scalar(c3(cols[:, 0, :]), ba[:, :, 0:8], -80.0, None, ALU.max))
                    link(v.tensor_tensor(c3(lp[:, 2, 0:16]), ba[:, :, 8:16], rowp[:, 1, :].unsqueeze(1).to_broadcast([P, TT, 8]), ALU.add))
                    link(v.tensor_scalar(lp[:, 2, 16:24], par[:, PCOL["lru_lambda"]:PCOL["lru_lambda"] + 8], -1.0, None, ALU.mult))
                    link(v.tensor_scalar(lp[:, 3, :], lp[:, 2, :], -1.0, None, ALU.mult))
                    v.tensor_tensor(lp[:, 0, :], lp[:, 2, :], lp[:, 3, :], ALU.min).then_inc(ln_in, 1)
                if t == 4:
                    dve.wait_ge(ln_out, 3)
                    link(v.tensor_scalar(lp[:, 3, :], lp[:, 1, :], 2.0, None, ALU.add))
                    link(v.reciprocal(lp[:, 4, :], lp[:, 3, :]))
                    link(v.tensor_tensor(lp[:, 3, :], lp[:, 1, :], lp[:, 4, :], ALU.mult))
                    link(v.tensor_tensor(lp[:, 4, :], lp[:, 3, :], lp[:, 3, :], ALU.mult))
                    link(v.tensor_scalar(lp[:, 5, :], lp[:, 4, :], 1.0 / 17, None, ALU.mult))
                    for m in (15, 13, 11, 9, 7, 5, 3):
                        link(v.scalar_tensor_tensor(lp[:, 5, :], lp[:, 5, :], 1.0 / m, lp[:, 4, :], ALU.add, ALU.mult))
                    link(v.scalar_tensor_tensor(lp[:, 5, :], lp[:, 5, :], 1.0, lp[:, 3, :], ALU.add, ALU.mult))
                    link(v.tensor_scalar(lp[:, 3, :], lp[:, 2, :], 0.0, None, ALU.max))
                    link(v.scalar_tensor_tensor(lp[:, 4, :], lp[:, 5, :], 2.0, lp[:, 3, :], ALU.mult, ALU.add))
                    for t in range(TT):
                        last = v.scalar_tensor_tensor(gg[:, t * 8:t * 8 + 8], lp[:, 4, t * 8:t * 8 + 8], -1.0, cols[:, 5, 0:8],
                                                      ALU.mult, ALU.mult)
                    last.then_inc(g_ready, 1)
                    link(v.tensor_scalar(lruc[:, 2, :], lp[:, 4, 16:24], -4.0, None, ALU.mult))
                    link(v.tensor_scalar(lruc[:, 0, :], par[:, PCOL["lru_br"]:PCOL["lru_br"] + 8], 0.5, None, ALU.mult))
                    link(v.tensor_scalar(lruc[:, 1, :], par[:, PCOL["lru_bi"]:PCOL["lru_bi"] + 8], 0.5, None, ALU.mult))
                    link(v.tensor_scalar(cols[:, 0, :], cols[:, 4, :], 1.0, None, ALU.add))
                    link(v.reciprocal(beta, cols[:, 0, :]))
                if t == 7:
                    dve.wait_ge(gc_done, 1)
                    link(v.tensor_copy(gc, B[4][:, 256:272]))
                    link(v.tensor_copy(cols[:, 1, :], gc))
                    v.tensor_tensor(cols[:, 2, :], B[4][:, 272:288], gc, ALU.subtract).then_inc(cols_in, 1)
                if t == 8:
                    dve.wait_ge(cols_out, 2)
                    link(v.tensor_tensor(bexp, cols[:, 4, :], beta, ALU.mult))

            def hyb_front(p, t):
                n = HYB + PAIR_TICKS * p + t
                j, gi = t // 4, 6 * p + t // 4
                if t == 11:
                    dve.wait_ge(gram_done, p + 1)
                    dve.wait_ge(qk_n, p + 1)
                    for u in range(4):
                        h, tt = 2 * p + u // 2, u % TT
                        s = slice(u * P, u * P + P)
                        last = v.tensor_scalar(W4[:, 3, s], B[1][:, s], gc[:, tt * 8 + h:tt * 8 + h + 1], 0.0, ALU.subtract, ALU.min)
                    last.then_inc(dmin, 1)
                if t == 10:
                    dve.wait_ge(qk_r, 2 * p + 2)
                    if p:
                        dve.wait_ge(os_done, 4 * p)
                        dve.wait_ge(uw_done, p)
                    v.tensor_tensor(qb[:], qb[:], W4[:, 2, :], ALU.mult)
                    v.tensor_tensor(kb[:], kb[:], W4[:, 3, :], ALU.mult)
                    for hh in range(2):
                        for buf, src in ((kbe, gg), (kdec, beta)):
                            s = c3(src)[:, :, 2 * p + hh:2 * p + hh + 1].to_broadcast([P, TT, P])
                            last = v.tensor_copy(buf[:, hh * TOK:hh * TOK + TOK].rearrange("p (t m) -> p t m", t=TT), s)
                    last.then_inc(qk_n, 1)
                if t == 12:
                    dve.wait_ge(dexp, 3 * p + 3)
                    r4 = lambda ap: ap.rearrange("p (u i) -> p u i", u=4)
                    v.tensor_tensor(LT[:], B[2][:], W4[:, 3, :], ALU.mult)
                    link(v.tensor_tensor(at[:], B[3][:], W4[:, 3, :], ALU.mult))
                    v.tensor_tensor(LT[:], LT[:], B[4][:], ALU.mult)
                    v.tensor_tensor(r4(at[:]), r4(at[:]), c_("tri").unsqueeze(1).to_broadcast([P, 4, P]), ALU.mult)
                    v.tensor_tensor(qd[:], qb[:], vb[:], ALU.mult).then_inc(lt_ready, 1)
                r4 = lambda ap: ap.rearrange("p (u i) -> p u i", u=4)
                mask = lambda name: c_(name).unsqueeze(1).to_broadcast([P, 4, P])
                if t == 13:
                    dve.wait_ge(lx_done, 6 * p + 1)
                    v.tensor_tensor(r4(W4[:, 0, :]), r4(B[2][:]), mask("level1"), ALU.mult)
                    link(v.tensor_tensor(r4(W4[:, 2, :]), r4(LT[:]), mask("level1T"), ALU.mult))
                    v.tensor_tensor(r4(W4[:, 1, :]), mask("ident"), r4(W4[:, 0, :]), ALU.subtract)
                    v.tensor_tensor(r4(W4[:, 2, :]), mask("ident"), r4(W4[:, 2, :]), ALU.subtract).then_inc(tu_ready, 1)
                if t in (3, 7, 13):
                    if t == 13:
                        j, gi, n = 2, gi - 1, n - 2
                    pad = pads[:, gi % 2]
                    if p:
                        if j < 2:
                            dve.wait_ge(lt_ready, p)
                        else:
                            dve.wait_ge(vT_done, p)
                    evac_scaled(pad[:, :, 3:3 + TOK], HYB, gi, n)
                    dve.wait_ge(group_evac, gi + 1)
                    tile = 8 * j + 2 * p
                    col = lambda k, b: slice(PCOL["gdn_conv_w"] + 24 * k + tile + b, PCOL["gdn_conv_w"] + 24 * k + tile + b + 1)
                    conv(pad, (qb, kb, vbuf)[j], None, col, 0, CONV).then_inc(conv_done, 1)
                level = (t - 12) // 2
                if t >= 14 and t % 2 == 0:
                    dve.wait_ge(lx_done, 6 * p + level + 1)
                    v.tensor_tensor(r4(W4[:, 0, :]), r4(B[2][:]), mask(f"level{2 ** level}"), ALU.mult).then_inc(x_masked, 1)
                if t == 19:
                    if p:
                        dve.wait_ge(lru_out, p)
                    evac_scaled(pads[:, gi % 2, :, 3:3 + TOK], HYB, gi, n)
                if t >= 15 and t % 2:
                    dve.wait_ge(tu_done, 5 * p + level)
                    dve.wait_ge(tu_ready, 6 * p + level)
                    if level < 5:
                        v.tensor_tensor(W4[:, 1, :], W4[:, 1, :], B[3][:], ALU.subtract)
                    v.tensor_tensor(W4[:, 2, :], W4[:, 2, :], B[4][:], ALU.subtract).then_inc(tu_ready, 1)
                if t == 15:
                    if p:
                        dve.wait_ge(gdn_out, p)
                    evac_scaled(two(zs[:]), HYB, gi, n)
                if t == 19:
                    pad = pads[:, gi % 2]
                    dve.wait_ge(group_evac, gi + 1)
                    cb, bb = PCOL["lru_conv_w"] + 2 * p, PCOL["lru_conv_b"] + 2 * p
                    conv(pad, xc, None, lambda k, b: slice(cb + 8 * k + b, cb + 8 * k + b + 1), 0, CONV,
                         bias=lambda b: slice(bb + b, bb + b + 1)).then_inc(xc_ready, 1)
                if t == 21:
                    dve.wait_ge(ri_tanh, p + 1)
                    for b in range(2):
                        s = slice(b * TOK, b * TOK + TOK)
                        last = v.tensor_scalar(rt[:, s], rt[:, s], 1.0, lruc[:, 2, 2 * p + b:2 * p + b + 1], ALU.add, ALU.mult)
                    last.then_inc(la_ready, 1)
                if t == 23:
                    evac_scaled(two(gl_), HYB, gi, n)

            def hyb_tail(p, t):
                if t == 0:
                    dve.wait_ge(uw_done, p + 1)
                    v.tensor_copy(usb[:], B[2][:]).then_inc(u_ready, 1)
                    dve.wait_ge(u_ready, p + 1)
                if t == 1:
                    dve.wait_ge(os_done, 4 * p + 1)
                    v.tensor_copy(St[:], B[4][:, 0:256]).then_inc(s_ready, 1)
                if t in (0, 2, 4, 6):
                    c = t // 2
                    rows = slice(64 * (c % 2), 64 * (c % 2) + 64)
                    hs = lambda ap, w: ap.rearrange("p (h x) -> p h x", h=2)[rows, :, w]
                    u3 = hs(usb[:], slice(c // 2 * P, c // 2 * P + P))
                    vn = vnew[rows, :].rearrange("p (h x) -> p h x", h=2)
                    if c == 0:
                        v.tensor_copy(vn, u3).then_inc(vn_ready, 1)
                    else:
                        dve.wait_ge(ws_done, 3 * p + c)
                        v.tensor_tensor(vn, u3, B[2][rows, 0:256].rearrange("p (h x) -> p h x", h=2), ALU.subtract).then_inc(vn_ready, 1)
                if t in (3, 5):
                    c = t // 2
                    dve.wait_ge(os_done, 4 * p + c + 1)
                    dve.wait_ge(s_ready, 3 * p + c)
                    for h in range(2):
                        s = slice(h * P, h * P + P)
                        last = v.scalar_tensor_tensor(St[:, s], St[:, s], egl[:, 4 * h + c:4 * h + c + 1], B[4][:, s],
                                                      ALU.mult, ALU.add)
                    last.then_inc(s_ready, 1)
                if t == 0:
                    dve.wait_ge(lru_ln, 4 * p + 4)
                    v.tensor_tensor(l2[:], l2[:], l1, ALU.subtract).then_inc(lru_dif, 1)
                if t == 1:
                    link(v.scalar_tensor_tensor(it[:], it[:], 1.0, xc[:], ALU.add, ALU.mult))
                if t == 2:
                    dve.wait_ge(lru_root, p + 1)
                    link(v.tensor_tensor(it[:], it[:], l2[:], ALU.mult))
                    for b in range(2):
                        s = slice(b * TOK, b * TOK + TOK)
                        last = v.tensor_tensor_scan(xc[:, s], rt[:, s], it[:, s], 0.0, ALU.mult, ALU.add)
                    link(last)
                if t == 3:
                    dve.wait_ge(gate_out, p + 1)
                    link(v.tensor_tensor(xc[:], xc[:], gl_, ALU.mult))
                    split_act(slice(8 + 2 * p, 10 + 2 * p), two(xc[:]), lru_out)
                if t == 8:
                    dve.wait_ge(o_r, p + 1)
                    dve.wait_ge(z_ready, p + 1)
                    link(v.tensor_tensor(ro[:], B[5][:], ro[:], ALU.mult))
                    link(v.scalar_tensor_tensor(ro[:], ro[:], pcol("gdn_norm", 0), zs[:], ALU.mult, ALU.mult))
                    split_act(slice(2 * p, 2 * p + 2), two(ro[:]), gdn_out)

            def mem_quarter(layer, j):
                dve.wait_ge(pieces_done, (MEM[0] - 4 + j if layer == 0 else XQ[0] + 4 + j) + 1)
                for g in (2 * j, 2 * j + 1):
                    if layer == 0:
                        dve.wait_ge(sq_ready, 8 * S_PHASE["mem0"] + g + 1)
                    else:
                        dve.wait_ge(mT_done, 4 + j + 1)
                    split_h(g, B[g % 2][:], "norm_mem", KT * layer)

            for p in range(PAIRS):
                for t in range(PAIR_TICKS):
                    split(HYB + PAIR_TICKS * p + t + AHEAD)
                    hyb_front(p, t)
                    if p:
                        hyb_tail(p - 1, t)
                    else:
                        gates(t)
                    if p == PAIRS - 1 and t >= 21:
                        mem_quarter(0, t - 21)

            def mem_side(layer, t):
                n0, s, r = ((qb, kb, vbuf) if layer == 0 else (nraw, nsq, nr))
                g = t // 4
                if t % 4 == 3:
                    if g:
                        if g < 3:
                            dve.wait_ge(n_out, N_MEM[layer] + g)
                        else:
                            dve.wait_ge(xvT, 2 * layer + g - 2)
                    evac_scaled(two(n0[:]), MEM[layer], GROUP[MEM[layer]] + g, MEM[layer] + t, rows=rstd_m)
                if t in (4, 8):
                    head_norm(N_MEM[layer] + g - 1, n0, r, s, B[0], xk[layer][:, 2 * (g - 1):2 * g, :], "xk_norm", layer)

            def head_norm(ni, src, r, s, bank, dst, gain, k):
                dve.wait_ge(n_r, ni + 1)
                link(refine(r[:], s[:], bank[:], X_HD))
                v.scalar_tensor_tensor(dst, two(src[:]), pcol(gain, k), two(r[:]), ALU.mult, ALU.mult).then_inc(n_out, 1)

            def residual(gi, g, n, gain, k):
                dve.wait_ge(pieces_done, n + 1)
                x2 = xT[:, 2 * g:2 * g + 2, :]
                v.tensor_tensor(x2, two(ST[gi % 2][:]), x2, ALU.add).then_inc(group_evac, 1)
                if gain:
                    dve.wait_ge(group_evac, gi + 1)
                    split_h(g, x2.rearrange("p k c -> p (k c)"), gain, k)

            def cross(layer):
                def negmax(h):
                    dve.wait_ge(xs_done, 4 * layer + h + 1)
                    link(v.tensor_reduce(xmx[:, h, 0:2], two(B[2 + h % 2][:]), AX.X, ALU.max))
                    v.tensor_scalar(xmx[:, h, 2:4], xmx[:, h, 0:2], -(X_HD ** -0.5), None, ALU.mult).then_inc(xneg, 1)

                def norm(h):
                    dve.wait_ge(xexp, 4 * layer + h + 1)
                    link(v.reciprocal(xmx[:, h, 0:2], xmx[:, h, 4:6]))
                    v.tensor_tensor(two(xp[:, h % 2]), two(xp[:, h % 2]), xmx[:, h, 0:2].unsqueeze(2).to_broadcast([P, 2, TOK]),
                                    ALU.mult).then_inc(xpn, 1)

                def outp(h):
                    dve.wait_ge(xo_done, 4 * layer + h + 1)
                    split_act(h, B[5][:, 0:TOK], xo_out)

                return negmax, norm, outp

            def ffn(layer):
                for b in range(2):
                    last = v.memset(gpad[:, 0, b, 0:2], 0.0)
                link(last)
                for c, size, tile, n, g0 in ffn_parts(layer):
                    cw = PCOL["ffn_conv_w"] + 3 * FT * layer + tile
                    cb = PCOL["ffn_conv_b"] + FT * layer + tile
                    done = (tile // 2) + layer * (FT // 2)
                    with dve.Fori(0, size // 2) as i:
                        link.start(i, 4)
                        for t in range(8):
                            split(n + t + AHEAD, i)
                            if t == 3:
                                evac_scaled(gpad[:, 0, :, 2:2 + TOK], 0, g0, n + 3, i)
                                dve.wait_ge(group_evac, g0 + 1 + 2 * i)
                                conv(gpad[:, 0], gcv[:, 0], None, lambda k, b: bass.ds(cw + FT * k + b + 2 * i, 1), 0, 3,
                                     bias=lambda b: bass.ds(cb + b + 2 * i, 1)).then_inc(gt_conv, 1)
                            if t == 7:
                                evac_scaled(two(fup[:]), 0, g0 + 1, n + 7, i)
                                dve.wait_ge(gt_silu, done + 1 + i)
                                dve.wait_ge(group_evac, g0 + 2 + 2 * i)
                                link(v.tensor_tensor(fup[:], fup[:], gcv[:, 0], ALU.mult))
                                split_act(bass.ds(2 * i, 2), two(fup[:]), ffn_act)
                        link.end(size // 2)
                    n += 4 * size
                    g0 += size
                    q = size // 4
                    for g in range(8):
                        for t in range(q):
                            split(n + g * q + t + AHEAD)
                        norm = c == 2 and layer == 0
                        residual(g0 + g, g, n + g * q + q - 1, "norm_mix" if norm else None, KT)

            def common(layer):
                def mixout(t):
                    split(MIXOUT[layer] + t + AHEAD)
                    g, q = mix_order(layer, t)
                    if q == 3:
                        residual(GROUP[MIXOUT[layer]] + g, g, MIXOUT[layer] + t, "norm_cross", KT * layer)

                first = 0
                if layer == 1:
                    for t in range(32, 41):
                        swa_first(t)
                        if t < 38:
                            mixout(t - 32)
                        swa_side(t)
                    first = 6
                for t in range(first, 32):
                    mixout(t)
                ni = N_XQ[layer]
                HB = B[1 if layer else 5]
                negmax, norm, outp = cross(layer)
                for t in range(8):
                    split(XQ[layer] + t + AHEAD)
                    if t == 1:
                        refine_rows(S_PHASE[f"mix{layer}"])
                    if t == 7:
                        dve.wait_ge(n_out, ni + 1)
                    if t in (3, 7):
                        evac_scaled(two(nraw[:]), 0, GROUP[XQ[layer]] + t // 4, XQ[layer] + t)
                    if t == 5:
                        head_norm(ni, nraw, nr, nsq, HB, xq[:, 0:2, :], "xq_norm", layer)
                    if layer and t == 6:
                        negmax(0)
                        negmax(1)
                    if layer and t == 7:
                        norm(0)
                    if layer == 0 and t >= 5:
                        mem_quarter(1, t - 5)
                if layer == 0:
                    for t in range(16):
                        split(MEM[1] + t + AHEAD)
                        if t == 0:
                            head_norm(ni + 1, nraw, nr, nsq, HB, xq[:, 2:4, :], "xq_norm", layer)
                            mem_quarter(1, 3)
                        if t == 1:
                            negmax(0)
                            negmax(1)
                        if t in (3, 5):
                            negmax((t + 1) // 2)
                        if t in (5, 7, 9, 11):
                            outp((t - 5) // 2)
                        if t in (2, 4, 6, 8):
                            norm(t // 2 - 1)
                        mem_side(1, t)
                else:
                    norm(1)
                    outp(0)
                    head_norm(ni + 1, nraw, nr, nsq, HB, xq[:, 2:4, :], "xq_norm", layer)
                    negmax(2)
                    outp(1)
                    negmax(3)
                    norm(2)
                    norm(3)
                    outp(2)
                    outp(3)
                for g in range(8):
                    split(XO[layer] + g + AHEAD)
                    residual(GROUP[XO[layer]] + g, g, XO[layer] + g, "norm_ffn", KT * layer)
                refine_rows(S_PHASE[f"xo{layer}"])
                ffn(layer)

            def rope(t, ni, gi, n, dst, gain, sem_out):
                r = ni - N_ROPE
                if t == 3:
                    if r in (1, 2):
                        dve.wait_ge(kT_done, r)
                    if r == 2:
                        dve.wait_ge(svT, 2)
                    if r > 2:
                        dve.wait_ge(q_rot, r - 2)
                    evac_scaled(two(nraw[:]), 0, gi, n)
                if t == 5:
                    dve.wait_ge(n_r, ni + 1)
                    link(refine(nr[:], nsq[:], B[0][:], SWA_HD))
                    v.scalar_tensor_tensor(two(nraw[:]), two(nraw[:]), pcol(gain, 0), two(nr[:]), ALU.mult, ALU.mult).then_inc(n_out, 1)
                if t == 6:
                    dve.wait_ge(rot_done, r + 1)
                    dve.wait_ge(trig_ready, 2)
                    v.tensor_tensor(two(nsq[:]), two(B[1][:]), sinb[:].unsqueeze(1).to_broadcast([P, 2, TOK]), ALU.mult)
                    link(v.tensor_tensor(two(nraw[:]), two(nraw[:]), cosb[:].unsqueeze(1).to_broadcast([P, 2, TOK]), ALU.mult))
                    v.tensor_tensor(dst, two(nraw[:]), two(nsq[:]), ALU.add).then_inc(sem_out, 1)

            def swa_first(t):
                g = (t - 9) // 4
                if 9 <= t and g < 8 and t == 4 * g + 9:
                    dve.wait_ge(s_exp, g + 1)
                    link(v.tensor_tensor(sst[:, 5, :], sst[:, 2, :], sst[:, 4, :], ALU.add))
                    link(v.reciprocal(sst[:, 5, :], sst[:, 5, :]))
                    v.tensor_tensor(sc[:, :, 0:P], sc[:, :, 0:P], sst[:, 5, 0:4].unsqueeze(2).to_broadcast([P, 4, P]), ALU.mult)
                    v.tensor_tensor(sc[:, :, P:384], sc[:, :, P:384], sst[:, 5, 4:8].unsqueeze(2).to_broadcast([P, 4, 256]),
                                    ALU.mult).then_inc(s_prob, 1)

            def swa_side(t):
                for lag in (3, 5, 6):
                    g = (t - lag) // 4
                    if t >= lag and g < 8 and t == 4 * g + lag:
                        if lag == 6 and g:
                            dve.wait_ge(s_done, g)
                        rope(lag, N_ROPE + 2 + g, GROUP[SWQ] + g, SWQ + t, two(qf[:]), "swa_q_norm", q_rot)
                g = (t - 7) // 4
                if 7 <= t and g < 8 and t == 4 * g + 7:
                    dve.wait_ge(s_done, g + 1)
                    if g:
                        dve.wait_ge(pt_done, g)
                    band = c_("band", 256)
                    v.scalar_tensor_tensor(sc[:, :, 0:P], B[2][:].rearrange("p (k c) -> p k c", k=4), SWA_HD ** -0.5,
                                           band[:, P:256].unsqueeze(1).to_broadcast([P, 4, P]), ALU.mult, ALU.add)
                    for b in range(2):
                        last = v.scalar_tensor_tensor(sc[:, 2 * b:2 * b + 2, P:384], two(B[3 + b][:]), SWA_HD ** -0.5,
                                                      band.unsqueeze(1).to_broadcast([P, 2, 256]), ALU.mult, ALU.add)
                    last.then_inc(s_masked, 1)
                    dve.wait_ge(s_masked, g + 1)
                    v.tensor_reduce(sst[:, 0, 0:4], sc[:, :, 0:P], AX.X, ALU.max)
                    link(v.tensor_reduce(sst[:, 0, 4:8], sc[:, :, P:384], AX.X, ALU.max))
                    sk = sinks[:, 4 * g:4 * g + 4].unsqueeze(1).to_broadcast([P, 2, 4])
                    s2_ = lambda k: sst[:, k, :].rearrange("p (n h) -> p n h", n=2)
                    link(v.tensor_tensor(s2_(0), s2_(0), sk, ALU.max))
                    link(v.tensor_scalar(sst[:, 1, :], sst[:, 0, :], -1.0, None, ALU.mult))
                    v.tensor_tensor(s2_(3), s2_(1), sk, ALU.add).then_inc(s_neg, 1)
                g = (t - 12) // 4
                if 12 <= t and g < 8 and t == 4 * g + 12:
                    dve.wait_ge(pv_done, g + 1)
                    split_act(slice(2 * g, 2 * g + 2), two(B[5][:]), swa_out)

            for t in range(16):
                split(MEM[0] + t + AHEAD)
                if t == 1:
                    refine_rows(S_PHASE["mem0"])
                hyb_tail(PAIRS - 1, t)
                if t == 0:
                    mem_quarter(0, 3)
                mem_side(0, t)
            common(0)
            dve.wait_ge(pos_loaded, 32)
            link(v.tensor_copy(ang[:, 2, :], posi[:]))
            link(v.tensor_scalar(ang[:, 0, :], ang[:, 2, :], c_("freq", 1), None, ALU.mult))
            link(v.tensor_scalar(ang[:, 1, :], ang[:, 0, :], 1.0 / (2 * math.pi), None, ALU.mult))
            link(v.tensor_scalar(ang[:, 1, :], ang[:, 1, :], 12582912.0, None, ALU.add))
            link(v.tensor_scalar(ang[:, 1, :], ang[:, 1, :], -12582912.0, None, ALU.add))
            c1 = 6.28125
            c2 = float(np.float32(2 * math.pi - c1).view(np.int32) & -4096) and float(
                (np.array(np.float32(2 * math.pi - c1)).view(np.int32) & -4096).view(np.float32))
            c3_ = 2 * math.pi - c1 - c2
            for part in (c1, c2, c3_):
                link(v.scalar_tensor_tensor(ang[:, 0, :], ang[:, 1, :], -part, ang[:, 0, :], ALU.mult, ALU.add))
            link(v.tensor_scalar(ang[:, 0, :], ang[:, 0, :], -3.1415925, 3.1415925, ALU.max, ALU.min))
            link(v.tensor_scalar(ang[:, 1, :], ang[:, 0, :], -1.0, None, ALU.mult))
            link(v.tensor_tensor(ang[:, 1, :], ang[:, 1, :], ang[:, 0, :], ALU.min))
            v.tensor_scalar(ang[:, 1, :], ang[:, 1, :], math.pi / 2, None, ALU.add).then_inc(ang_ready, 1)
            refine_rows(S_PHASE["ffn0"])
            for t in range(16):
                split(SWKV + t + AHEAD)
                g, k = t // 4, t % 4
                if g < 2 and k == 3:
                    rope(3, N_ROPE + g, GROUP[SWKV] + g, SWKV + t, None, "swa_k_norm", kT_done)
                if t in (5, 9):
                    rope(5, N_ROPE + g - 1, 0, 0, None, "swa_k_norm", kT_done)
                if t in (6, 10):
                    rope(6, N_ROPE + g - 1, 0, 0, kTt[:, 2 * (g - 1):2 * g, :], "swa_k_norm", kT_done)
                if t in (11, 15):
                    dve.wait_ge(kT_done, 2)
                    if t == 15:
                        dve.wait_ge(svT, 1)
                    evac_scaled(two(nraw[:]), 0, GROUP[SWKV] + g, SWKV + t)
            for t in range(32):
                swa_first(t)
                split(SWQ + t + AHEAD)
                swa_side(t)
            common(1)

        @block.tensor
        def _(pe):
            mm = nc.tensor.matmul

            def transpose(o, i):
                return nc.tensor.transpose(o, i, ident)

            def piece(n, gi, q, last_q, rhi, rlo, kts, i=0, g_i=0):
                k = n % NSPLIT
                pe.wait_ge(lo_split, n + 1 + 8 * i)
                if q == 0 and gi >= 2:
                    pe.wait_ge(group_evac, gi - 1 + g_i)
                bank = ST[gi % 2]
                for m in range(2):
                    for kk, kt in enumerate(kts):
                        o = bank[:, m * TOK:m * TOK + TOK]
                        w = slice(m * P, m * P + P)
                        first = q == 0 and m == 0 and kk == 0
                        final = q == last_q and kk == len(kts) - 1
                        mm(o, whi[:, k, kk, w], rhi[:, kt, :], start=first, stop=False, skip_group_check=True)
                        mm(o, whi[:, k, kk, w], rlo[:, kt, :], start=False, stop=False, skip_group_check=True)
                        last = mm(o, wlo[:, k, kk, w], rhi[:, kt, :], start=False, stop=final, skip_group_check=True)
                last.then_inc(pieces_done, 1)

            def tick(start, t, rhi, rlo, quarters=4, ready=None):
                g, q = t // quarters, t % quarters
                if ready:
                    ready(q)
                piece(start + t, GROUP[start] + g, q, quarters - 1, rhi, rlo, range(NK * q, NK * q + NK))

            def h_is(phase):
                return lambda q: pe.wait_ge(h_ready, 8 * H_PHASE[phase] + 2 * q + 2)

            def sum_squares(name, g, sq, bank):
                phase = S_PHASE[name]
                pe.wait_ge(sq_ready, 8 * phase + g + 1)
                if g == 0 and phase:
                    pe.wait_ge(rstd_ready, phase)
                for b in range(2):
                    last = mm(bank[:, 0:TOK], ones, (sq[g % 2] if isinstance(sq, list) else sq[:, g % 2])[:, b * TOK:b * TOK + TOK], start=(g == 0 and b == 0),
                              stop=(g == 7 and b == 1), skip_group_check=True)
                last.then_inc(ss_done, 1)

            pe.wait_ge(c_loaded, 16)
            def param_tile(j):
                n = min(P, PARAM_ROWS - j * P)
                if j >= 2:
                    pe.wait_ge(par_ready, j - 1)
                nc.tensor.transpose(B[3 + j % 2][:, 0:n], prow[0:n, j, :], ident[0:n, 0:n]).then_inc(prowT, 1)

            pe.wait_ge(gain_loaded, 16 * GAIN_DMAS)
            param_tile(0)
            pe.wait_ge(x_loaded, 32)
            for g in range(8):
                if g >= 2:
                    pe.wait_ge(xt_copied, g - 1)
                    pe.wait_ge(sq_ready, g - 1)
                for b in range(2):
                    for t in range(TT):
                        o = b * TOK + t * P
                        last = transpose(B[1 + g % 2][:, o:o + P], x_tok[:, t, (2 * g + b) * P:(2 * g + b) * P + P])
                last.then_inc(xtT, 1)
                if g:
                    sum_squares("x", g - 1, sq0, B[0])
            sum_squares("x", 7, sq0, B[0])

            def gates(t):
                if t == 0:
                    pe.wait_ge(p_loaded, 16 * P_DMAS)
                    for j in range(1, PARAM_TILES):
                        param_tile(j)
                if t == 2:
                    pe.wait_ge(par_ready, PARAM_TILES)
                    pe.wait_ge(rstd_ready, 1)
                    for k in range(TT):
                        last = transpose(B[4][:, k * P:k * P + P], rstd[:, k * P:k * P + P])
                    last.then_inc(rtok_ready, 1)
                    pe.wait_ge(ba_split, 1)
                    pe.wait_ge(h_ready, 8)
                    for k in range(TT):
                        o = B[3][:, k * 16:k * 16 + 16]
                        s = slice(k * P, k * P + P)
                        for kt in range(KT):
                            mm(o, hhi[:, kt, s], wbah[:, kt, :], start=(kt == 0), stop=False, skip_group_check=True)
                            mm(o, hhi[:, kt, s], wbal[:, kt, :], start=False, stop=False, skip_group_check=True)
                            last = mm(o, hlo[:, kt, s], wbah[:, kt, :], start=False, stop=(kt == KT - 1), skip_group_check=True)
                    last.then_inc(ba_done, 1)
                if t == 7:
                    pe.wait_ge(g_ready, 1)
                    mm(B[4][:, 256:272], c_("tri"), gg, start=True, stop=True)
                    mm(B[4][:, 272:288], c_("chunk"), gg, start=True, stop=True).then_inc(gc_done, 1)

            def units(bank, lhs, rhs):
                for u in range(4):
                    s = slice(u * P, u * P + P)
                    last = mm(bank[:, s], lhs[:, s], rhs if rhs.shape[1] == P else rhs[:, s], start=True, stop=True)
                return last

            def hyb_front(p, t):
                if t == 9:
                    pe.wait_ge(qk_sq, 2 * p + 2)
                    mm(B[0][:], ones, W4[:, 0, :], start=True, stop=True)
                    mm(B[1][:], ones, W4[:, 1, :], start=True, stop=True).then_inc(qk_ss, 1)
                if t == 11:
                    pe.wait_ge(qk_n, p + 1)
                    if p == 0:
                        pe.wait_ge(cols_in, 1)
                    units(B[2], kb, kb)
                    units(B[3], kb, qb)
                    for u in range(4):
                        transpose(B[0][:, u * P:u * P + P], kb[:, u * P:u * P + P])
                    units(B[1], kbe, c_("tri"))
                    for u in range(4):
                        last = transpose(B[4][:, u * P:u * P + P], kdec[:, u * P:u * P + P])
                    last.then_inc(gram_done, 1)
                if t == 15:
                    pe.wait_ge(silu_done, 3 * p + 3)
                    pe.wait_ge(dexp, 3 * p + 3)
                    for u in range(4):
                        last = transpose(B[1][:, u * P:u * P + P], vbuf[:, u * P:u * P + P])
                    last.then_inc(vT_done, 1)
                if t == 13:
                    pe.wait_ge(lt_ready, p + 1)
                    for u in range(4):
                        last = transpose(B[2][:, u * P:u * P + P], LT[:, u * P:u * P + P])
                    last.then_inc(lx_done, 1)
                level = (t - 12) // 2
                if t >= 14 and t % 2 == 0:
                    pe.wait_ge(tu_ready, 6 * p + level)
                    units(B[2], LT, W4[:, 1, :]).then_inc(lx_done, 1)
                if t >= 15 and t % 2:
                    pe.wait_ge(x_masked, 5 * p + level)
                    if level < 5:
                        units(B[3], W4[:, 2, :], W4[:, 0, :])
                    units(B[4], W4[:, 0, :], W4[:, 2, :]).then_inc(tu_done, 1)
                if t == 20:
                    pe.wait_ge(xc_ready, p + 1)
                    pe.wait_ge(kt_scaled, p + 1)
                    pe.wait_ge(vb_ready, p + 1)
                    for w_, bank in ((wr, B[0]), (wi, B[1])):
                        for b in range(2):
                            last = mm(bank[:, b * TOK:b * TOK + TOK], w_[:, 2 * p + b, :], xc[:, b * TOK:b * TOK + TOK],
                                      start=True, stop=True)
                    last.then_inc(ri_done, 1)

            def hyb_tail(p, t):
                if t == 0:
                    pe.wait_ge(tu_ready, 6 * p + 6)
                    pe.wait_ge(kt_scaled, p + 1)
                    pe.wait_ge(vb_ready, p + 1)
                    for u in range(4):
                        s = slice(u * P, u * P + P)
                        mm(B[2][:, s], W4[:, 2, s], vb[:, s], start=True, stop=True)
                        last = mm(B[3][:, s], kbe[:, s], W4[:, 2, s], start=True, stop=True)
                    last.then_inc(uw_done, 1)
                c = t // 2
                if t in (2, 4, 6):
                    rows = slice(64 * (c % 2), 64 * (c % 2) + 64)
                    pe.wait_ge(s_ready, 3 * p + c)
                    if c == 1:
                        pe.wait_ge(w_ready, p + 1)
                    for h in range(2):
                        i0 = h * TOK + c * CHUNK
                        last = mm(B[2][rows, h * P:h * P + P], wsb[:, i0:i0 + CHUNK], St[:, h * P:h * P + P],
                                  start=True, stop=True)
                    last.then_inc(ws_done, 1)
                if t in (1, 3, 5, 7):
                    tt, half = c // 2, c % 2
                    rows = slice(64 * half, 64 * half + 64)
                    pe.wait_ge(vn_ready, 4 * p + c + 1)
                    if c == 0 and p:
                        pe.wait_ge(gdn_out, p)
                    if c == 0 and p == PAIRS - 1:
                        pe.wait_ge(rstd_ready, S_PHASE["mem0"] + 1)
                    for h in range(2):
                        i0 = h * TOK + c * CHUNK
                        o = B[5][:, i0:i0 + CHUNK]
                        if c:
                            mm(o, St[:, h * P:h * P + P], qd[:, i0:i0 + CHUNK], start=False, stop=False, skip_group_check=True)
                        u0 = (2 * h + tt) * P
                        last = mm(o, vnew[rows, h * P:h * P + P], at[rows, u0 + 64 * half:u0 + 64 * half + CHUNK],
                                  start=(c == 0 and h == 0), stop=(c == 3), skip_group_check=True)
                        if c < 3:
                            last = mm(B[4][:, h * P:h * P + P], kdec[rows, u0:u0 + P], vnew[rows, h * P:h * P + P],
                                      start=True, stop=True)
                    last.then_inc(os_done, 1)
                if t == 8:
                    pe.wait_ge(o_sq, p + 1)
                    mm(B[4][:], ones, osq, start=True, stop=True).then_inc(o_ss, 1)

            def mem_sums(j):
                for g in (2 * j, 2 * j + 1):
                    sum_squares("mem0", g, msq, B[5])

            def mem_quarter(layer, j):
                pe.wait_ge(m_loaded, 16 * (4 * layer + j + 1))
                if j:
                    pe.wait_ge(h_ready, 8 * H_PHASE[f"mem{layer}"] + 2 * j)
                elif layer == 0:
                    pe.wait_ge(ri_tanh, PAIRS)
                    pe.wait_ge(gdn_out, PAIRS - 1)
                else:
                    pe.wait_ge(rstd_ready, S_PHASE["mix0"] + 1)
                    pe.wait_ge(xv_ready, 2)
                for gg_ in range(2):
                    for b in range(2):
                        for t in range(TT):
                            o = b * TOK + t * P
                            last = transpose(B[gg_][:, o:o + P], stage[:, t, (2 * gg_ + b) * P:(2 * gg_ + b) * P + P])
                last.then_inc(mT_done, 1)

            for p in range(PAIRS):
                for t in range(PAIR_TICKS):
                    if p == 0 and t < 4:
                        h_is("x")(t)
                    piece(HYB + PAIR_TICKS * p + t, 6 * p + t // 4, t % 4, 3, hhi, hlo, range(4 * (t % 4), 4 * (t % 4) + 4))
                    hyb_front(p, t)
                    if p:
                        hyb_tail(p - 1, t)
                    else:
                        gates(t)
                    if p == PAIRS - 1 and t >= 21:
                        if t > 21:
                            mem_sums(t - 22)
                        mem_quarter(0, t - 21)

            def head_ss(ni, s, bank, w=None):
                pe.wait_ge(n_sq, ni + 1)
                if ni:
                    pe.wait_ge(n_out, ni)
                mm(bank[:], w if w is not None else ones, s[:], start=True, stop=True).then_inc(n_ss, 1)

            def mem_side(layer, t):
                n0, s, r = ((qb, kb, vbuf) if layer == 0 else (nraw, nsq, nr))
                g = t // 4
                if t in (4, 8):
                    head_ss(N_MEM[layer] + g - 1, s, B[0])
                if t in (12, 16):
                    pe.wait_ge(group_evac, GROUP[MEM[layer]] + g)
                    if g == 4:
                        pe.wait_ge(xv_ready, 2 * layer + 1)
                    for tt in range(TT):
                        for b in range(2):
                            last = transpose(B[1][:, (tt * 2 + b) * P:(tt * 2 + b) * P + P],
                                             n0[:, b * TOK + tt * P:b * TOK + tt * P + P])
                    last.then_inc(xvT, 1)

            def cross(layer):
                def scores(h):
                    if h in (0, 2):
                        pe.wait_ge(n_out, N_XQ[layer] + 1 + h // 2)
                    if h >= 2:
                        pe.wait_ge(xexp, 4 * layer + h - 1)
                    for u in range(2):
                        last = mm(B[2 + h % 2][:, u * TOK:u * TOK + TOK], xq[:, h, u * P:u * P + P], xk[layer][:, h, :],
                                  start=True, stop=True)
                    last.then_inc(xs_done, 1)

                def turn(h):
                    pe.wait_ge(xpn, 4 * layer + h + 1)
                    if h:
                        pe.wait_ge(xpt_copied, 4 * layer + h)
                    for u in range(2):
                        for m in range(2):
                            last = transpose(B[4][:, m * TOK + u * P:m * TOK + u * P + P],
                                             xp[:, h % 2, u * TOK + m * P:u * TOK + m * P + P])
                    last.then_inc(xpt_done, 1)

                def pv(h):
                    pe.wait_ge(xpt_copied, 4 * layer + h + 1)
                    if h:
                        pe.wait_ge(xo_out, 4 * layer + h)
                    for m in range(2):
                        last = mm(B[5][:, 0:TOK], xv[layer][:, m, h, :], xpT[:, h % 2, m * TOK:m * TOK + TOK],
                                  start=(m == 0), stop=(m == 1))
                    last.then_inc(xo_done, 1)

                return scores, turn, pv

            def common(layer):
                def mix_ready(q):
                    if layer:
                        pe.wait_ge(swa_out, 2 * q + 2)
                    elif q < 2:
                        pe.wait_ge(gdn_out, 2 * q + 2)
                    else:
                        pe.wait_ge(lru_out, 2 * q - 2)

                mix, xo = f"mix{layer}", f"xo{layer}"

                def mixout(t):
                    g, q = mix_order(layer, t)
                    mix_ready(q)
                    piece(MIXOUT[layer] + t, GROUP[MIXOUT[layer]] + g, q, 3, ahi, alo, range(NK * q, NK * q + NK))

                if layer == 1:
                    for t in range(32, 41):
                        if t < 38:
                            mixout(t - 32)
                        swa_side(t)
                for t in range(6 * layer, 32):
                    mixout(t)
                    if layer == 0 and t == 0:
                        mem_side(0, 16)
                    g = {7: 0, 8: 1}.get(t) if layer and t <= 8 else t // 4 - 1 if t % 4 == 0 and t else None
                    if g is not None:
                        if g == 0:
                            pe.wait_ge(n_out, N_XQ[layer])
                        sum_squares(mix, g, xsq, B[0])
                sum_squares(mix, 7, xsq, B[0])
                ni = N_XQ[layer]
                HB = B[1 if layer else 5]
                scores, turn, pv = cross(layer)
                for t in range(8):
                    tick(XQ[layer], t, hhi, hlo, ready=h_is(mix))
                    if t == 4:
                        head_ss(ni, nsq, HB)
                    if layer and t == 6:
                        scores(0)
                        scores(1)
                    if layer and t == 7:
                        turn(0)
                    if layer == 0 and t >= 5:
                        mem_quarter(1, t - 5)
                if layer == 0:
                    for t in range(16):
                        tick(MEM[1], t, hhi, hlo, ready=h_is("mem1"))
                        if t == 0:
                            head_ss(ni + 1, nsq, HB)
                            mem_quarter(1, 3)
                        if t == 1:
                            scores(0)
                            scores(1)
                        if t in (5, 7, 9, 11):
                            pv((t - 5) // 2)
                        if t in (3, 5, 7, 9):
                            turn((t - 3) // 2)
                        if t in (3, 5):
                            scores((t + 1) // 2)
                        mem_side(1, t)
                else:
                    head_ss(ni + 1, nsq, HB)
                    pv(0)
                    turn(1)
                    scores(2)
                    pv(1)
                    scores(3)
                    turn(2)
                    pv(2)
                    turn(3)
                    pv(3)
                pe.wait_ge(xo_out, 4 * layer + 4)
                for g in range(8):
                    piece(XO[layer] + g, GROUP[XO[layer]] + g, 0, 0, ahi, alo, range(4))
                    if layer == 0 and g == 0:
                        mem_side(1, 16)
                    if g:
                        if g == 1:
                            pe.wait_ge(n_out, 6 + 12 * layer)
                        sum_squares(xo, g - 1, xsq, B[0])
                sum_squares(xo, 7, xsq, B[0])
                ffn(layer)

            def ffn(layer):
                ph = H_PHASE[f"xo{layer}"]
                for c, size, tile, n, g0 in ffn_parts(layer):
                    done = (tile // 2) + layer * (FT // 2)
                    with pe.Fori(0, size // 2) as i:
                        for half in range(2):
                            for q in range(4):
                                if c == 0:
                                    pe.wait_ge(h_ready, 8 * ph + 2 * q + 2)
                                piece(n + 4 * half + q, g0 + half, q, 3, hhi, hlo, range(4 * q, 4 * q + 4), i, 2 * i)
                    n += 4 * size
                    g0 += size
                    q_ = size // 4
                    for g in range(8):
                        for q in range(q_):
                            pe.wait_ge(ffn_act, done + 2 * q + 2)
                            piece(n + g * q_ + q, g0 + g, q, q_ - 1, ahi, alo, range(4 * q, 4 * q + 4))
                            if c == 2 and q == 0 and g:
                                if layer == 0:
                                    sum_squares("ffn0", g - 1, xsq, B[0])
                                else:
                                    out_turn(g0, g - 1)
                    if c == 2 and layer == 0:
                        sum_squares("ffn0", 7, xsq, B[0])
                    if c == 2 and layer == 1:
                        out_turn(g0, 7)

            def out_turn(g0, g):
                pe.wait_ge(group_evac, g0 + g + 1)
                if g >= 2:
                    pe.wait_ge(o_staged, g - 1)
                for b in range(2):
                    for t in range(TT):
                        o = b * TOK + t * P
                        last = transpose(B[1 + g % 2][:, o:o + P], xT[:, 2 * g + b, t * P:t * P + P])
                last.then_inc(oT_done, 1)

            def rope(t, ni):
                if t == 4:
                    head_ss(ni, nsq, B[0], c_("half"))
                if t == 6:
                    pe.wait_ge(n_out, ni + 1)
                    mm(B[1][:], c_("rot"), nraw[:], start=True, stop=True).then_inc(rot_done, 1)

            def swa_side(t):
                g = (t - 10) // 4
                if 10 <= t and g < 8 and t == 4 * g + 10:
                    pe.wait_ge(s_prob, g + 1)
                    for i in range(4):
                        for b in range(3):
                            k = 3 * i + b
                            last = transpose(B[2 + k // 4][:, (k % 4) * P:(k % 4) * P + P], sc[:, i, b * P:b * P + P])
                    last.then_inc(pt_done, 1)
                for lag in (4, 6):
                    g = (t - lag) // 4
                    if t >= lag and g < 8 and t == 4 * g + lag:
                        rope(lag, N_ROPE + 2 + g)
                g = (t - 11) // 4
                if 11 <= t and g < 8 and t == 4 * g + 11:
                    pe.wait_ge(pt_copied, g + 1)
                    if g:
                        pe.wait_ge(swa_out, g)
                    for i in range(4):
                        rows = slice(64 * (i % 2), 64 * (i % 2) + 64)
                        vk = lambda tt: vtok[:, tt, g // 2, 64 * (g % 2):64 * (g % 2) + 64]
                        o = i // 2 * TOK
                        mm(B[5][rows, o:o + P], vk(0), pT[:, 3 * i, :], start=True, stop=True)
                        mm(B[5][rows, o + P:o + TOK], vk(0), pT[:, 3 * i + 1, :], start=True, stop=False)
                        last = mm(B[5][rows, o + P:o + TOK], vk(1), pT[:, 3 * i + 2, :], start=False, stop=True)
                    last.then_inc(pv_done, 1)
                g = (t - 7) // 4
                if 7 <= t and g < 8 and t == 4 * g + 7:
                    pe.wait_ge(q_rot, g + 1)
                    if g == 0:
                        pe.wait_ge(ksw_ready, 2)
                        pe.wait_ge(sv_ready, 2)
                    for i in (0, 2, 1, 3):
                        half = i % 2
                        if i == 1:
                            pe.wait_ge(even_heads, g + 1)
                        rows = slice(64 * half, 64 * half + 64)
                        kk_ = (kTt if half == g % 2 else kTs)[rows, g // 2, :]
                        q0 = i // 2 * TOK
                        mm(B[2][:, i * P:i * P + P], qf[rows, q0:q0 + P], kk_[:, 0:P], start=True, stop=True)
                        last = mm(B[3 + i // 2][:, half * TOK:half * TOK + TOK], qf[rows, q0 + P:q0 + TOK], kk_, start=True, stop=True)
                        if i == 2:
                            last.then_inc(even_heads, 1)
                    last.then_inc(s_done, 1)

            def swa_v(j):
                pe.wait_ge(group_evac, GROUP[SWKV] + 3 + j)
                pe.wait_ge(n_out, N_ROPE + 2)
                if j:
                    pe.wait_ge(sv_ready, 1)
                for tt in range(TT):
                    for b in range(2):
                        last = transpose(B[0][:, (tt * 2 + b) * P:(tt * 2 + b) * P + P], nraw[:, b * TOK + tt * P:b * TOK + tt * P + P])
                last.then_inc(svT, 1)

            for t in range(16):
                tick(MEM[0], t, hhi, hlo, ready=h_is("mem0"))
                if t == 0:
                    mem_sums(2)
                    mem_quarter(0, 3)
                hyb_tail(PAIRS - 1, t)
                if t == 0:
                    mem_sums(3)
                mem_side(0, t)
            common(0)
            for t in range(16):
                tick(SWKV, t, hhi, hlo, ready=h_is("ffn0"))
                g = t // 4
                if t in (4, 8):
                    pe.wait_ge(rstd_ready, S_PHASE["ffn0"] + 1)
                    rope(4, N_ROPE + g - 1)
                if t in (6, 10):
                    rope(6, N_ROPE + g - 1)
                if t in (7, 11):
                    pe.wait_ge(kT_done, g)
                    if g == 2:
                        pe.wait_ge(ksw_ready, 1)
                    mm(B[2][:], c_("swap"), kTt[:, 2 * (g - 1):2 * g, :], start=True, stop=True).then_inc(ksw_done, 1)
                if t == 12:
                    swa_v(0)
            for t in range(32):
                tick(SWQ, t, hhi, hlo, ready=h_is("ffn0"))
                if t == 0:
                    swa_v(1)
                swa_side(t)
            common(1)


_INS = ["x", "mem", "positions", "norm_mix", "norm_cross", "norm_mem", "norm_ffn", "xq_w", "xkv_w", "xo_w",
        "xq_norm", "xk_norm", "ffn_in_w", "ffn_conv_w", "ffn_conv_b", "ffn_out_w", "hyb_in_w", "hyb_out_w",
        "gdn_conv_w", "gdn_a_log", "gdn_dt_bias", "gdn_norm", "lru_conv_w", "lru_conv_b", "lru_wr", "lru_br",
        "lru_wi", "lru_bi", "lru_lambda", "swa_in_w", "swa_out_w", "swa_q_norm", "swa_k_norm", "swa_sinks"]


def kernel(**inputs):
    import concourse.bacc as _bacc
    from concourse.bass_utils import run_bass_kernel_spmd as _run

    nc = _bacc.Bacc("TRN2", target_bir_lowering=False, num_devices=1)
    arrays = {f"in_{name}": np.ascontiguousarray(inputs[name]) for name in _INS}
    arrays["in_consts"] = constants()
    handles = {}
    for name, arr in arrays.items():
        handles[name[3:]] = nc.dram_tensor(name, arr.shape, mybir.dt.from_np(arr.dtype), kind="ExternalInput").ap()
    out = nc.dram_tensor("out_0", (1, TOK, D), F32, kind="ExternalOutput").ap()
    trunk(nc, handles, out)
    return _run(nc, [arrays], core_ids=[0]).results[0]["out_0"]
```
